# Optimizing a Trainium2 kernel written in Bass

```python
import jax, jax.numpy as jnp
from jax import lax
import numpy as np

D_MODEL = 1024
BATCH = 1
SEQ = 2048
DEPTH = 2

CTX_LEN = 256
GRID_W = 64
HEAD_DIM = 64
D_CONV = 256
CONV_WIDTH = 31
N_DN_HEADS = 6
D_DN = N_DN_HEADS * HEAD_DIM
SHORT_CONV = 5
DN_CHUNK = 64
N_Q_HEADS = 6
N_KV_HEADS = 2
D_ATTN = N_Q_HEADS * HEAD_DIM
D_KV = N_KV_HEADS * HEAD_DIM
WINDOW = 128
ATTN_BLOCK = 128
ROPE_BASE = 10000.0
D_MIX = D_CONV + D_DN + D_ATTN
N_IN = 3 * D_CONV + 4 * D_DN + 4 * N_DN_HEADS + 2 * D_ATTN + 2 * D_KV
EPS = 1e-6

kernel_name = "hymba_style_conv_deltanet_swa_dit"

def _rmsnorm(x, w):
    xf = x.astype(jnp.float32)
    y = xf * lax.rsqrt(jnp.mean(xf * xf, axis=-1, keepdims=True) + EPS)
    return (y * w.astype(jnp.float32)).astype(x.dtype)

def _layernorm(x, w, b):
    xf = x.astype(jnp.float32)
    mu = jnp.mean(xf, axis=-1, keepdims=True)
    var = jnp.mean(jnp.square(xf - mu), axis=-1, keepdims=True)
    y = (xf - mu) * lax.rsqrt(var + EPS) * w.astype(jnp.float32) + b.astype(jnp.float32)
    return y.astype(x.dtype)

def _l2norm(x):
    return x * lax.rsqrt(jnp.sum(x * x, axis=-1, keepdims=True) + EPS)

def _depthwise_conv(x, w):
    k = w.shape[0]
    pad = (k - 1) // 2
    return lax.conv_general_dilated(
        x, w[:, None, :].astype(x.dtype), window_strides=(1,), padding=[(pad, k - 1 - pad)],
        dimension_numbers=('NWC', 'WIO', 'NWC'), feature_group_count=x.shape[-1])

def _ada(cond, w, b):
    m = jax.nn.silu(cond) @ w + b
    return jnp.split(m, 3, axis=-1)

def _split_cols(p):
    sizes = (D_CONV, D_CONV, D_CONV,
             D_DN, D_DN, D_DN, D_DN,
             4 * N_DN_HEADS,
             D_ATTN, D_KV, D_KV, D_ATTN)
    idx = np.cumsum(sizes)[:-1].tolist()
    return jnp.split(p, idx, axis=-1)

def _axial_rope(t, rows, cols):
    d = t.shape[-1]
    half, quarter = d // 2, d // 4
    inv = ROPE_BASE ** (-jnp.arange(quarter, dtype=jnp.float32) / quarter)

    def rot(th, pos):
        ang = pos.astype(jnp.float32)[:, None] * inv
        cos = jnp.cos(ang)[None, :, None, :].astype(t.dtype)
        sin = jnp.sin(ang)[None, :, None, :].astype(t.dtype)
        x1, x2 = th[..., :quarter], th[..., quarter:]
        return jnp.concatenate([x1 * cos - x2 * sin, x2 * cos + x1 * sin], axis=-1)

    return jnp.concatenate([rot(t[..., :half], rows), rot(t[..., half:], cols)], axis=-1)

def _conformer_conv(a_val, a_gate, z, conv_w, conv_b, ln_w, ln_b):
    u = a_val * jax.nn.sigmoid(a_gate)
    u = _depthwise_conv(u, conv_w) + conv_b
    u = jax.nn.silu(_layernorm(u, ln_w, ln_b))
    return u * jax.nn.silu(z)

def _gdn_inputs(q, k, v, sc, conv_w, a_log, dt_bias):
    b_, l_ = q.shape[:2]
    qkv = jax.nn.silu(_depthwise_conv(jnp.concatenate([q, k, v], axis=-1), conv_w)).astype(jnp.float32)
    q, k, v = jnp.split(qkv, 3, axis=-1)
    q = _l2norm(q.reshape(b_, l_, N_DN_HEADS, HEAD_DIM))
    k = _l2norm(k.reshape(b_, l_, N_DN_HEADS, HEAD_DIM))
    v = v.reshape(b_, l_, N_DN_HEADS, HEAD_DIM)
    sc = sc.astype(jnp.float32).reshape(b_, l_, 2, 2, N_DN_HEADS)
    beta = jax.nn.sigmoid(sc[:, :, :, 0])
    g = -jnp.exp(a_log.astype(jnp.float32)) * jax.nn.softplus(sc[:, :, :, 1] + dt_bias.astype(jnp.float32))
    return q, k, v, g, beta

def _gdn_chunk_scan(q, k, v, g, beta, s0, with_out):
    b_, l_, h_, dk = q.shape
    dv = v.shape[-1]
    n = l_ // DN_CHUNK

    def chunked(t):
        t = t.reshape((b_, n, DN_CHUNK, h_) + t.shape[3:])
        return jnp.moveaxis(jnp.moveaxis(t, 1, 0), 3, 2)

    qc = chunked(q) * dk ** -0.5
    kc, vc = chunked(k), chunked(v)
    bc = chunked(beta)
    gc = jnp.cumsum(chunked(g), axis=-1)
    idx = jnp.arange(DN_CHUNK)
    strict = idx[:, None] > idx[None, :]
    incl = idx[:, None] >= idx[None, :]
    diff = gc[..., :, None] - gc[..., None, :]
    kb = kc * bc[..., None]
    lmat = jnp.einsum('nbhid,nbhjd->nbhij', kb, kc) * jnp.exp(jnp.where(strict, diff, -jnp.inf))
    amat = lmat + jnp.eye(DN_CHUNK, dtype=lmat.dtype)
    rhs = jnp.concatenate([vc * bc[..., None], kb * jnp.exp(gc)[..., None]], axis=-1)
    sol = lax.linalg.triangular_solve(amat, rhs, left_side=True, lower=True, unit_diagonal=True)
    u, w = sol[..., :dv], sol[..., dv:]
    g_last = gc[..., -1]
    k_dec = kc * jnp.exp(g_last[..., None] - gc)[..., None]
    xs = (u, w, k_dec, g_last)
    if with_out:
        intra = jnp.einsum('nbhid,nbhjd->nbhij', qc, kc) * jnp.exp(jnp.where(incl, diff, -jnp.inf))
        q_dec = qc * jnp.exp(gc)[..., None]
        xs = xs + (q_dec, intra)

    def step(s, xs_i):
        u_i, w_i, kd_i, gl_i = xs_i[:4]
        v_new = u_i - jnp.einsum('bhck,bhkv->bhcv', w_i, s)
        s_new = s * jnp.exp(gl_i)[..., None, None] + jnp.einsum('bhck,bhcv->bhkv', kd_i, v_new)
        if with_out:
            qd_i, a_i = xs_i[4:]
            o_i = jnp.einsum('bhck,bhkv->bhcv', qd_i, s) + jnp.einsum('bhij,bhjv->bhiv', a_i, v_new)
            return s_new, o_i
        return s_new, None

    s_fin, o = lax.scan(step, s0, xs)
    if with_out:
        o = jnp.moveaxis(jnp.moveaxis(o, 2, 3), 0, 1).reshape(b_, l_, h_, dv)
    return o, s_fin

def _gdn_bidir(q, k, v, g, beta, s0_f, s0_b, with_out):
    flip = lambda t: jnp.flip(t, axis=1)
    o_f, s_f = _gdn_chunk_scan(q, k, v, g[:, :, 0], beta[:, :, 0], s0_f, with_out)
    o_b, s_b = _gdn_chunk_scan(flip(q), flip(k), flip(v), flip(g[:, :, 1]), flip(beta[:, :, 1]), s0_b, with_out)
    o = o_f + flip(o_b) if with_out else None
    return o, s_f, s_b

def _gated_head_norm(o, z, w, dtype):
    b_, l_ = o.shape[:2]
    return _rmsnorm(o.astype(dtype), w).reshape(b_, l_, D_DN) * jax.nn.silu(z)

def _softmax_with_sink(scores, sink):
    s = jnp.broadcast_to(sink[None, :, :, None, None], scores.shape[:-1] + (1,))
    p = jax.nn.softmax(jnp.concatenate([scores, s], axis=-1), axis=-1)
    return p[..., :-1]

def _latent_attention(q, k, v, k_ctx, v_ctx, sink):
    b_, l_, hq, d = q.shape
    group = hq // N_KV_HEADS
    nb = l_ // ATTN_BLOCK
    span = ATTN_BLOCK + 2 * WINDOW
    scale = d ** -0.5
    qg = q.reshape(b_, nb, ATTN_BLOCK, N_KV_HEADS, group, d)
    pad = ((0, 0), (WINDOW, WINDOW), (0, 0), (0, 0))
    kp, vp = jnp.pad(k, pad), jnp.pad(v, pad)
    offs_q = jnp.arange(ATTN_BLOCK)
    offs_k = jnp.arange(span) - WINDOW
    band = jnp.abs(offs_k[None, :] - offs_q[:, None]) <= WINDOW
    sink_g = sink.reshape(N_KV_HEADS, group).astype(jnp.float32)

    def one_block(i):
        q_i = qg[:, i]
        k_i = lax.dynamic_slice_in_dim(kp, i * ATTN_BLOCK, span, axis=1)
        v_i = lax.dynamic_slice_in_dim(vp, i * ATTN_BLOCK, span, axis=1)
        kpos = i * ATTN_BLOCK + offs_k
        valid = band & ((kpos >= 0) & (kpos < l_))[None, :]
        s_loc = jnp.einsum('bqhgd,bkhd->bhgqk', q_i, k_i).astype(jnp.float32) * scale
        s_loc = jnp.where(valid, s_loc, -jnp.inf)
        s_ctx = jnp.einsum('bqhgd,bkhd->bhgqk', q_i, k_ctx).astype(jnp.float32) * scale
        p = _softmax_with_sink(jnp.concatenate([s_loc, s_ctx], axis=-1), sink_g).astype(v.dtype)
        return (jnp.einsum('bhgqk,bkhd->bqhgd', p[..., :span], v_i)
                + jnp.einsum('bhgqk,bkhd->bqhgd', p[..., span:], v_ctx))

    out = lax.map(one_block, jnp.arange(nb))
    return jnp.moveaxis(out, 0, 1).reshape(b_, l_, hq * d)

def _context_attention(q, k, v, sink):
    b_, lc, hq, d = q.shape
    group = hq // N_KV_HEADS
    qg = q.reshape(b_, lc, N_KV_HEADS, group, d)
    s = jnp.einsum('bqhgd,bkhd->bhgqk', qg, k).astype(jnp.float32) * d ** -0.5
    p = _softmax_with_sink(s, sink.reshape(N_KV_HEADS, group).astype(jnp.float32)).astype(v.dtype)
    return jnp.einsum('bhgqk,bkhd->bqhgd', p, v).reshape(b_, lc, hq * d)

def _hybrid_layer(x, xc, c3, cc3, rows, cols, norm_w, ada_w, ada_b, w_in, conv_a_w, conv_a_b,
                  ln_a_w, ln_a_b, qkv_conv_w, a_log, dt_bias, dn_norm_w, sink, w_out, with_ctx_out):
    b_, l_ = x.shape[:2]
    lc = xc.shape[1]
    shift, scale, gate = _ada(c3, ada_w, ada_b)
    shift_c, scale_c, gate_c = _ada(cc3, ada_w, ada_b)
    h = _rmsnorm(x, norm_w) * (1.0 + scale) + shift
    hc = _rmsnorm(xc, norm_w) * (1.0 + scale_c) + shift_c
    (a_val, a_gate, z_a, q_b, k_b, v_b, z_b, sc_b, q_c, k_c, v_c, z_c) = _split_cols(h @ w_in)
    (a_val_x, a_gate_x, z_a_x, q_b_x, k_b_x, v_b_x, z_b_x, sc_b_x,
     q_c_x, k_c_x, v_c_x, z_c_x) = _split_cols(hc @ w_in)

    y_a = _conformer_conv(a_val, a_gate, z_a, conv_a_w, conv_a_b, ln_a_w, ln_a_b)

    s0 = jnp.zeros((b_, N_DN_HEADS, HEAD_DIM, HEAD_DIM), jnp.float32)
    gin_x = _gdn_inputs(q_b_x, k_b_x, v_b_x, sc_b_x, qkv_conv_w, a_log, dt_bias)
    o_bx, s_f, s_b = _gdn_bidir(*gin_x, s0, s0, with_ctx_out)
    gin = _gdn_inputs(q_b, k_b, v_b, sc_b, qkv_conv_w, a_log, dt_bias)
    o_b, _, _ = _gdn_bidir(*gin, s_f, s_b, True)
    y_b = _gated_head_norm(o_b, z_b, dn_norm_w, x.dtype)

    k_ctx = k_c_x.reshape(b_, lc, N_KV_HEADS, HEAD_DIM)
    v_ctx = v_c_x.reshape(b_, lc, N_KV_HEADS, HEAD_DIM)
    q_lat = _axial_rope(q_c.reshape(b_, l_, N_Q_HEADS, HEAD_DIM), rows, cols)
    k_lat = _axial_rope(k_c.reshape(b_, l_, N_KV_HEADS, HEAD_DIM), rows, cols)
    v_lat = v_c.reshape(b_, l_, N_KV_HEADS, HEAD_DIM)
    y_c = _latent_attention(q_lat, k_lat, v_lat, k_ctx, v_ctx, sink) * jax.nn.silu(z_c)

    y = jnp.concatenate([y_a, y_b, y_c], axis=-1) @ w_out
    x = x + gate * y

    if with_ctx_out:
        y_ax = _conformer_conv(a_val_x, a_gate_x, z_a_x, conv_a_w, conv_a_b, ln_a_w, ln_a_b)
        y_bx = _gated_head_norm(o_bx, z_b_x, dn_norm_w, xc.dtype)
        q_ctx = q_c_x.reshape(b_, lc, N_Q_HEADS, HEAD_DIM)
        y_cx = _context_attention(q_ctx, k_ctx, v_ctx, sink) * jax.nn.silu(z_c_x)
        yc = jnp.concatenate([y_ax, y_bx, y_cx], axis=-1) @ w_out
        xc = xc + gate_c * yc
    return x, xc

def setup_inputs(seed: int = 0) -> dict:
    key = jax.random.key(seed)
    ks = jax.random.split(key, 20)
    f32 = jnp.float32
    nrm = lambda k, s: jax.random.normal(k, s, f32)
    dt = jnp.exp(jax.random.uniform(ks[12], (DEPTH, 2, N_DN_HEADS), f32)
                 * (np.log(0.1) - np.log(0.001)) + np.log(0.001))
    return {
        "x": nrm(ks[0], (BATCH, SEQ, D_MODEL)),
        "c": nrm(ks[1], (BATCH, D_MODEL)),
        "ctx": nrm(ks[2], (BATCH, CTX_LEN, D_MODEL)),
        "c_ctx": nrm(ks[3], (D_MODEL,)),
        "norm_w": 1.0 + 0.1 * nrm(ks[4], (DEPTH, D_MODEL)),
        "ada_w": nrm(ks[5], (DEPTH, D_MODEL, 3 * D_MODEL)) * (0.5 * D_MODEL ** -0.5),
        "ada_b": 0.02 * nrm(ks[6], (DEPTH, 3 * D_MODEL)),
        "w_in": nrm(ks[7], (DEPTH, D_MODEL, N_IN)) * D_MODEL ** -0.5,
        "conv_a_w": nrm(ks[8], (DEPTH, CONV_WIDTH, D_CONV)) * CONV_WIDTH ** -0.5,
        "conv_a_b": 0.02 * nrm(ks[9], (DEPTH, D_CONV)),
        "ln_a_w": 1.0 + 0.1 * nrm(ks[10], (DEPTH, D_CONV)),
        "ln_a_b": 0.02 * nrm(ks[11], (DEPTH, D_CONV)),
        "qkv_conv_w": nrm(ks[13], (DEPTH, SHORT_CONV, 3 * D_DN)) * SHORT_CONV ** -0.5,
        "a_log": jnp.log(jax.random.uniform(ks[14], (DEPTH, 2, N_DN_HEADS), f32, 1.0, 16.0)),
        "dt_bias": dt + jnp.log(-jnp.expm1(-dt)),
        "dn_norm_w": 1.0 + 0.1 * nrm(ks[15], (DEPTH, HEAD_DIM)),
        "sink": nrm(ks[16], (DEPTH, N_Q_HEADS)),
        "w_out": nrm(ks[17], (DEPTH, D_MIX, D_MODEL)) * D_MIX ** -0.5,
        "final_norm_w": 1.0 + 0.1 * nrm(ks[18], (D_MODEL,)),
    }

def reference(x, c, ctx, c_ctx, norm_w, ada_w, ada_b, w_in, conv_a_w, conv_a_b, ln_a_w, ln_a_b,
              qkv_conv_w, a_log, dt_bias, dn_norm_w, sink, w_out, final_norm_w):
    n_tok = x.shape[1]
    n_rows = n_tok // GRID_W
    rows = jnp.repeat(jnp.arange(n_rows, dtype=jnp.int32), GRID_W)
    cols = jnp.tile(jnp.arange(GRID_W, dtype=jnp.int32), n_rows)
    c3 = c[:, None, :]
    cc3 = c_ctx[None, None, :]
    xc = ctx
    for l in range(DEPTH):
        x, xc = _hybrid_layer(x, xc, c3, cc3, rows, cols, norm_w[l], ada_w[l], ada_b[l], w_in[l],
                              conv_a_w[l], conv_a_b[l], ln_a_w[l], ln_a_b[l], qkv_conv_w[l],
                              a_log[l], dt_bias[l], dn_norm_w[l], sink[l], w_out[l],
                              l < DEPTH - 1)
    return _rmsnorm(x, final_norm_w)


_drawn_inputs = setup_inputs


def setup_inputs(seed=0):
    import zlib

    import numpy as np

    out = dict(_drawn_inputs(seed))
    spreads = {}
    factors = {'ctx': 3.769,
     'ada_b': 3.452,
     'conv_a_b': 8.0,
     'ln_a_w': 5.465,
     'ln_a_b': 31.009,
     'dn_norm_w': 3.092,
     'sink': 41.333}
    for name, (base, spread) in spreads.items():
        noise = np.random.default_rng([zlib.crc32(name.encode()), seed]).standard_normal(out[name].shape)
        drawn = base * np.exp(spread * noise) if base else spread * noise
        out[name] = __import__('jax').numpy.asarray(drawn.astype(out[name].dtype))
    for name, factor in factors.items():
        out[name] = (out[name] * factor).astype(out[name].dtype)
    return out
```

```python
from contextlib import ExitStack

import numpy as np

import concourse.bass as bass
from concourse import mybir

F32 = mybir.dt.float32
ALU = mybir.AluOpType
ACT = mybir.ActivationFunctionType
AX = mybir.AxisListType

P = 128
D = 1024
KT = D // P
DEPTH = 2
CTX, SEQ = 256, 2048
TOK = CTX + SEQ
NT = TOK // P
NCT = CTX // P
HD = 64
NH = 6
NP3 = NH // 2
CW_A, CW_B = 31, 5
PADC = (CW_A - 1) // 2
RL = 2352
C0 = PADC
L0 = PADC + CTX + PADC
CONV_N = CTX + PADC + SEQ
KPAD = P
EPS = 1e-6
CH = 64
NSTEP = TOK // CH
NCSTEP = CTX // CH
NEG = -1.0e30

S_A = 0
S_QKV = 12
S_QC = 21
S_KC, S_VC, S_SC = 24, 25, 26
NS = 27
Z_SLICE = [2, 3, 4, 5, 8, 9, 10, 11]
A_CONV = [0, 6]

GROUPS = [(0, CTX, C0)] + [(CTX + 512 * g, 512, L0 + 512 * g) for g in range(SEQ // 512)]
NG = len(GROUPS)


class Steps:

    def __init__(self, eng, sem, at=0):
        self.eng, self.sem, self.at, self.n = eng, sem, at, 0

    def inc(self, ins):
        self.n += 1
        return ins.then_inc(self.sem, 1)

    def link(self, ins):
        self.inc(ins)
        self.eng.wait_ge(self.sem, self.at + self.n)


class Mem:

    def __init__(self, nc, tag):
        self.nc, self.tag, self.stack, self.taken = nc, tag, ExitStack(), []

    def __enter__(self):
        self.stack.__enter__()
        return self

    def __exit__(self, *a):
        self.stack.__exit__(*a)
        self.nc.clear_and_free_semaphores(self.taken)
        self.nc.all_engine_barrier()

    def sb(self, name, *shape):
        return self.stack.enter_context(self.nc.sbuf_tensor(f"{self.tag}_{name}", [P, *shape], F32))

    def ps(self, name, *shape):
        return self.stack.enter_context(self.nc.psum_tensor(f"{self.tag}_{name}", [P, *shape], F32))

    def sem(self, name):
        self.taken.append(self.nc.alloc_semaphore(f"{self.tag}_{name}"))
        return self.taken[-1]

    def sems(self, name, n):
        return [self.sem(f"{name}{i}") for i in range(n)]

    def block(self):
        return self.stack.enter_context(self.nc.Block())


def ds1(i):
    return bass.ds(i, 1)


def modulation(nc, t):
    NB = 3 * D // 512
    with Mem(nc, "ada") as m:
        cond = m.sb("cond", KT, 2)
        scond = m.sb("scond", KT, 2)
        w = [m.sb(f"w{b}", KT, 512) for b in range(2)]
        bias = m.sb("bias", DEPTH, 3 * D)
        out = [m.sb(f"out{b}", 512) for b in range(2)]
        acc = m.ps("acc", 2, 512)
        in_loaded, cond_ready = m.sem("in_loaded"), m.sem("cond_ready")
        w_loaded, out_stored = m.sems("w_loaded", 2), m.sems("out_stored", 2)
        acc_ready, out_ready = m.sem("acc_ready"), m.sem("out_ready")
        blk = m.block()
        n_it = DEPTH * NB
        w_src = t["ada_w"]

        @blk.sync
        def _(sp):
            sp.dma_start(cond[:], t["cond"]).then_inc(in_loaded, 16)
            sp.dma_start(bias[0:2], t["ada_b"]).then_inc(in_loaded, 16)
            for b in range(2):
                sp.dma_start(w[b][:], w_src[b]).then_inc(w_loaded[b], 16)
            for b in range(2):
                sp.sem_inc(out_stored[b], 16)
            def store(it, b):
                sp.wait_ge(out_ready, it + 1)
                sp.dma_start(t["mod"][ds1(it)].rearrange("a c n -> c (a n)"), out[b][0:2]).then_inc(out_stored[b], 16)

            with sp.Fori(0, n_it // 2 - 1) as i:
                for b in range(2):
                    store(i * 2 + b, b)
                    sp.dma_start(w[b][:], w_src[ds1(i * 2 + b + 2)].rearrange("a p k n -> p (a k) n")).then_inc(w_loaded[b], 16)
            for b in range(2):
                store(n_it - 2 + b, b)
            for b in range(2):
                sp.wait_ge(out_stored[b], 16 * (n_it // 2 + 1))

        @blk.scalar
        def _(act):
            act.wait_ge(in_loaded, 32)
            act.activation(scond[:], cond[:], ACT.Silu).then_inc(cond_ready, 1)

        @blk.tensor
        def _(pe):
            pe.wait_ge(cond_ready, 1)
            with pe.Fori(0, n_it // 2) as i:
                for b in range(2):
                    pe.wait_ge(w_loaded[b], 16 * (i + 1))
                    for k in range(KT):
                        mm = pe.matmul(acc[0:2, b, :], scond[:, k, :], w[b][:, k, :], start=(k == 0), stop=(k == KT - 1))
                    mm.then_inc(acc_ready, 1)

        @blk.vector
        def _(dve):
            dve.wait_ge(in_loaded, 32)
            for it in range(n_it):
                b = it % 2
                dve.wait_ge(acc_ready, it + 1)
                dve.wait_ge(out_stored[b], 16 * (it // 2 + 1))
                dve.tensor_tensor(out[b][0:2], acc[0:2, b, :], bias[0:2, it // NB, 512 * (it % NB):512 * (it % NB) + 512],
                                  ALU.add).then_inc(out_ready, 1)


def normalise(nc, t, lay, hT, x_src):
    with Mem(nc, f"nrm{lay}") as m:
        ident = m.sb("ident", P)
        nw = m.sb("nw", KT)
        scale, shift, wsc = m.sb("scale", 2, KT), m.sb("shift", 2, KT), m.sb("wsc", 2, KT)
        eps = m.sb("eps", 1)
        x = [m.sb(f"x{b}", D) for b in range(2)]
        sq = m.sb("sq", D)
        ss = [m.sb(f"ss{b}", 1) for b in range(2)]
        lns = [m.sb(f"lns{b}", 1) for b in range(2)]
        rstd = [m.sb(f"rstd{b}", 1) for b in range(2)]
        xn = [m.sb(f"xn{b}", D) for b in range(2)]
        tp = m.ps("tp", 2, KT, P)
        par_loaded, const_ready = m.sem("par_loaded"), m.sem("const_ready")
        x_loaded = m.sems("x_loaded", 2)
        rstd_ready, xn_ready, tp_ready = m.sem("rstd_ready"), m.sem("xn_ready"), m.sem("tp_ready")
        act_own, dve_out, act_out = m.sem("act_own"), m.sem("dve_out"), m.sem("act_out")
        blk = m.block()
        n_act = KT // 2

        @blk.sync
        def _(sp):
            sp.dma_start(ident[:], t["ident"]).then_inc(par_loaded, 16)
            sp.dma_start(nw[:], t["norm_w"][lay]).then_inc(par_loaded, 16)
            for c in range(2):
                for k in range(2):
                    src = t["mod"][6 * lay + 2 * k:6 * lay + 2 * k + 2, c:c + 1, :]
                    for a in range(2):
                        sp.dma_start((shift, scale)[k][:, c, 4 * a:4 * a + 4], src[a, 0].rearrange("(k p) -> p k", p=P),
                                     allow_slow_non_contiguous=True).then_inc(par_loaded, 16)
            with sp.Fori(0, NT // 2) as i:
                for b in range(2):
                    sp.wait_ge(xn_ready, 2 * i + 1 + b)
                    sp.dma_start(x[b][:], x_src[bass.ds((i * 2 + b) * P, P), :]).then_inc(x_loaded[b], 16)

        @blk.vector
        def _(dve):
            dve.memset(eps[:], EPS).then_inc(const_ready, 1)
            dve.sem_inc(xn_ready, 2)
            dve.wait_ge(par_loaded, 10 * 16)
            for c in range(2):
                dve.scalar_tensor_tensor(wsc[:, c, :], scale[:, c, :], 1.0, nw[:], ALU.add, ALU.mult).then_inc(const_ready, 1)
            dve.wait_ge(const_ready, 3)
            for c, lo, hi in ((0, 0, NCT // 2), (1, NCT // 2, NT // 2)):
                with dve.Fori(lo, hi) as i:
                    for b in range(2):
                        dve.wait_ge(rstd_ready, 2 * i + b + 1)
                        dve.wait_ge(tp_ready, 2 * i + b + 1)
                        dve.tensor_scalar(xn[b][:], x[b][:], rstd[b][:], None, ALU.mult).then_inc(xn_ready, 1)
                        dve.wait_ge(tp_ready, 2 * i + b + 3)
                        for k in range(n_act, KT):
                            ins = dve.tensor_scalar(hT[:, k, bass.ds((i * 2 + b) * P, P)], tp[:, b, k, :],
                                                    wsc[:, 1 - c, k:k + 1], shift[:, 1 - c, k:k + 1], ALU.mult, ALU.add)
                        ins.then_inc(dve_out, 1)

        def tile_act(act, i, c):
            for b in range(2):
                s = Steps(act, act_own, (2 * i + b) * 2)
                act.wait_ge(x_loaded[b], 16 * (i + 1))
                s.link(act.activation(sq[:], x[b][:], ACT.Square, accum_out=ss[b][:]))
                s.link(act.activation(lns[b][:], ss[b][:], ACT.Ln, scale=1.0 / D, bias=eps[:]))
                act.activation(rstd[b][:], lns[b][:], ACT.Exp, scale=-0.5).then_inc(rstd_ready, 1)
                act.wait_ge(tp_ready, 2 * i + b + 3)
                for k in range(n_act):
                    ins = act.activation(hT[:, k, bass.ds((i * 2 + b) * P, P)], tp[:, b, k, :], ACT.Identity,
                                         scale=wsc[:, c, k:k + 1], bias=shift[:, c, k:k + 1])
                ins.then_inc(act_out, 1)

        @blk.scalar
        def _(act):
            act.wait_ge(const_ready, 3)
            with act.Fori(0, NCT // 2) as i:
                tile_act(act, i, 1)
            with act.Fori(NCT // 2, NT // 2) as i:
                tile_act(act, i, 0)

        @blk.tensor
        def _(pe):
            pe.sem_inc(tp_ready, 2)
            pe.sem_inc(dve_out, 2)
            pe.sem_inc(act_out, 2)
            pe.wait_ge(par_loaded, 10 * 16)
            with pe.Fori(0, NT // 2) as i:
                for b in range(2):
                    pe.wait_ge(xn_ready, 2 * i + b + 3)
                    pe.wait_ge(dve_out, 2 * i + b + 1)
                    pe.wait_ge(act_out, 2 * i + b + 1)
                    for k in range(KT):
                        mm = pe.transpose(tp[:, b, k, :], xn[b][:, k * P:(k + 1) * P], ident[:])
                    mm.then_inc(tp_ready, 1)


def project_slice(pe, s, w, hT, acc, acc_free, acc_ready):
    for g, (t0, n, _) in enumerate(GROUPS):
        pe.wait_ge(acc_free, s * NG + g + 1)
        for k in range(KT):
            mm = pe.matmul(acc[:, g, 0:n], w[:, k, :], hT[:, k, t0:t0 + n], start=(k == 0), stop=(k == KT - 1))
        mm.then_inc(acc_ready, 1)
    return mm


def take_out(act, s, acc, acc_ready, acc_free, row, func):
    for g, (_, n, col) in enumerate(GROUPS):
        act.wait_ge(acc_ready, s * NG + g + 1)
        ins = act.activation(row[:, col:col + n], acc[:, g, 0:n], func)
        ins.then_inc(acc_free, 1)
    return ins


def zero_pads(eng, rows, sem):
    for r in rows:
        for lo, hi in ((0, C0), (C0 + CTX, L0), (L0 + SEQ, RL)):
            eng.memset(r[:, lo:hi], 0.0).then_inc(sem, 1)


def project_a(nc, t, lay, hT):
    with Mem(nc, f"pa{lay}") as m:
        w = [m.sb(f"w{b}", KT, P) for b in range(2)]
        val, gate, u, conv = (m.sb(n, RL) for n in ("val", "gate", "u", "conv"))
        z = [m.sb(f"z{b}", RL) for b in range(2)]
        taps = m.sb("taps", 2, CW_A + 1)
        acc = m.ps("acc", NG, 512)
        w_loaded, z_stored = m.sems("w_loaded", 2), m.sems("z_stored", 2)
        taps_loaded, pads = m.sem("taps_loaded"), m.sem("pads")
        acc_ready, acc_free, row_ready = m.sem("acc_ready"), m.sem("acc_free"), m.sem("row_ready")
        u_ready, conv_own, conv_ready, conv_stored = (m.sem(n) for n in ("u_ready", "conv_own", "conv_ready", "conv_stored"))
        blk = m.block()
        rows = t["rows"]
        NI = 6

        @blk.sync
        def _(sp):
            sp.dma_start(taps[:], t["conv_a"][lay]).then_inc(taps_loaded, 16)
            for b in range(2):
                sp.dma_start(w[b][:], t["w_in"][lay, b]).then_inc(w_loaded[b], 16)
            with sp.Fori(0, 2) as i:
                for j in range(NI):
                    s = i * NI + j
                    sp.wait_ge(acc_ready, (s + 1) * NG)
                    sp.dma_start(w[j % 2][:], t["w_in"][lay, ds1(s + 2)].rearrange("a p k n -> p (a k) n")).then_inc(w_loaded[j % 2], 16)
                    if j >= 2:
                        sp.wait_ge(row_ready, s + 1)
                        sp.dma_start(rows[ds1(s)].rearrange("a p n -> p (a n)"), z[j % 2][:]).then_inc(z_stored[j % 2], 16)
                sp.wait_ge(conv_ready, i + 1)
                sp.dma_start(rows[ds1(i * NI)].rearrange("a p n -> p (a n)"), conv[:]).then_inc(conv_stored, 16)
            sp.wait_ge(conv_stored, 3 * 16)
            for b in range(2):
                sp.wait_ge(z_stored[b], 5 * 16)
                sp.wait_ge(w_loaded[b], 7 * 16)

        @blk.tensor
        def _(pe):
            pe.sem_inc(acc_free, NG)
            with pe.Fori(0, 2) as i:
                for j in range(NI):
                    pe.wait_ge(w_loaded[j % 2], 16 * (i * (NI // 2) + j // 2 + 1))
                    project_slice(pe, i * NI + j, w[j % 2], hT, acc, acc_free, acc_ready)

        @blk.scalar
        def _(act):
            for b in range(2):
                act.sem_inc(z_stored[b], 16)
            act.sem_inc(u_ready, 1)
            act.wait_ge(pads, 6 * 3)
            with act.Fori(0, 2) as i:
                for j in range(NI):
                    if j == 0:
                        act.wait_ge(u_ready, i + 1)
                    if j >= 2:
                        act.wait_ge(z_stored[j % 2], 16 * (i * 2 + (j - 2) // 2 + 1))
                    row, func = ((val, ACT.Copy), (gate, ACT.Sigmoid))[j] if j < 2 else (z[j % 2], ACT.Silu)
                    ins = take_out(act, i * NI + j, acc, acc_ready, acc_free, row, func)
                    act.wait_ge(acc_free, (i * NI + j + 2) * NG)
                    act.sem_inc(row_ready, 1)

        @blk.gpsimd
        def _(pool):
            zero_pads(pool, (val, gate, u, conv, *z), pads)
            pool.wait_ge(pads, 6 * 3)
            with pool.Fori(0, 2) as i:
                pool.wait_ge(row_ready, i * NI + 2)
                pool.wait_ge(conv_own, i * CW_A)
                pool.tensor_tensor(u[:, C0:C0 + CONV_N], val[:, C0:C0 + CONV_N], gate[:, C0:C0 + CONV_N], ALU.mult).then_inc(u_ready, 1)

        @blk.vector
        def _(dve):
            dve.sem_inc(conv_stored, 16)
            dve.wait_ge(taps_loaded, 16)
            dve.wait_ge(pads, 6 * 3)
            for i in range(2):
                dve.wait_ge(u_ready, i + 2)
                dve.wait_ge(conv_stored, 16 * (i + 1))
                s = Steps(dve, conv_own, i * CW_A)
                out = conv[:, C0:C0 + CONV_N]
                s.link(dve.tensor_scalar(out, u[:, 0:CONV_N], taps[:, i, 0:1], taps[:, i, CW_A:CW_A + 1], ALU.mult, ALU.add))
                for k in range(1, CW_A):
                    s.link(dve.scalar_tensor_tensor(out, u[:, k:k + CONV_N], taps[:, i, k:k + 1], out, ALU.mult, ALU.add))
                dve.sem_inc(conv_ready, 1)


NB_N = 3


def project_qkv(nc, t, lay, hT):
    with Mem(nc, f"pq{lay}") as m:
        w = [m.sb(f"w{b}", KT, P) for b in range(3)]
        raw = [m.sb(f"raw{b}", RL) for b in range(3)]
        con = [m.sb(f"con{b}", RL) for b in range(3)]
        rn = m.sb("rn", RL)
        taps = m.sb("taps", 9, CW_B)
        heads = m.sb("heads", P)
        eps = m.sb("eps", 2)
        acc = m.ps("acc", NG, 512)
        nps = m.ps("nps", NB_N, 512)
        w_loaded = m.sems("w_loaded", 3)
        stored = m.sems("stored", 3)
        par_loaded, pads = m.sem("par_loaded"), m.sem("pads")
        acc_ready, acc_free, row_ready = m.sem("acc_ready"), m.sem("acc_free"), m.sem("row_ready")
        dve_own, conv_ready, silu_ready, sq_ready = (m.sem(n) for n in ("dve_own", "conv_ready", "silu_ready", "sq_ready"))
        norm_ready, ln_ready, rn_ready, unit_ready = (m.sem(n) for n in ("norm_ready", "ln_ready", "rn_ready", "unit_ready"))
        blk = m.block()
        rows = t["rows"]
        wide = slice(C0, C0 + CONV_N)
        DVE_OWN = 3 * CW_B + 2
        OFF = (CW_A - CW_B) // 2

        @blk.sync
        def _(sp):
            sp.dma_start(taps[:], t["conv_b"][lay]).then_inc(par_loaded, 16)
            sp.dma_start(heads[:], t["blockdiag"]).then_inc(par_loaded, 16)
            for j in range(3):
                sp.dma_start(w[j][:], t["w_in"][lay, S_QKV + j]).then_inc(w_loaded[j], 16)
            with sp.Fori(0, 3) as i:
                for j in range(3):
                    s = i * 3 + j
                    sp.wait_ge(acc_ready, (s + 1) * NG)
                    sp.dma_start(w[j][:], t["w_in"][lay, ds1(s + S_QKV + 3)].rearrange("a p k n -> p (a k) n")).then_inc(w_loaded[j], 16)
                for j in range(3):
                    if j < 2:
                        sp.wait_ge(unit_ready, 2 * i + j + 1)
                    else:
                        sp.wait_ge(silu_ready, 3 * i + 3)
                    sp.dma_start(rows[ds1(i * 3 + (S_QKV + j))].rearrange("a p n -> p (a n)"), (con, con, raw)[j][j][:]).then_inc(stored[j], 16)
            for j in range(3):
                sp.wait_ge(stored[j], 4 * 16)
                sp.wait_ge(w_loaded[j], 4 * 16)

        @blk.tensor
        def _(pe):
            pe.sem_inc(acc_free, NG)
            pe.wait_ge(par_loaded, 32)

            def norms(n, j):
                pe.wait_ge(sq_ready, n + 1)
                for g, (_, cnt, col) in enumerate(GROUPS):
                    q = n * NG + g
                    pe.wait_ge(ln_ready, q + 1)
                    pe.matmul(nps[:, g % NB_N, 0:cnt], heads[:], con[j][:, col:col + cnt],
                              start=True, stop=True).then_inc(norm_ready, 1)

            pe.sem_inc(ln_ready, 2)
            with pe.Fori(0, 3) as i:
                for j in range(3):
                    pe.wait_ge(w_loaded[j], 16 * (i + 1))
                    project_slice(pe, i * 3 + j, w[j], hT, acc, acc_free, acc_ready)
                    if j >= 1:
                        norms(i * 2 + j - 1, j - 1)

        @blk.scalar
        def _(act):
            for j in range(3):
                act.sem_inc(stored[j], 16)
            act.wait_ge(pads, 6 * 3 + 2 + 1)

            def take(i, j):
                if j == 2:
                    act.wait_ge(stored[2], 16 * (i + 1))
                else:
                    act.wait_ge(dve_own, i * DVE_OWN)
                take_out(act, i * 3 + j, acc, acc_ready, acc_free, raw[j], ACT.Copy)
                act.wait_ge(acc_free, (i * 3 + j + 2) * NG)
                act.sem_inc(row_ready, 1)

            def silu(i, j):
                act.wait_ge(conv_ready, i * 3 + j + 1)
                act.activation(raw[j][:, C0:C0 + CTX], con[j][:, C0:C0 + CTX], ACT.Silu)
                act.activation(raw[j][:, L0:L0 + SEQ], con[j][:, L0:L0 + SEQ], ACT.Silu).then_inc(silu_ready, 1)

            def inverse_norm(i, j):
                if j == 1:
                    act.wait_ge(unit_ready, 2 * i + 1)
                else:
                    act.wait_ge(unit_ready, 2 * i)
                for g, (_, n, col) in enumerate(GROUPS):
                    q = (i * 2 + j) * NG + g
                    act.wait_ge(norm_ready, q + 1)
                    act.activation(rn[:, col:col + n], nps[:, g % NB_N, 0:n], ACT.Ln,
                                   scale=(float(HD), 1.0)[j], bias=eps[:, j:j + 1]).then_inc(ln_ready, 1)
                act.wait_ge(ln_ready, (i * 2 + j + 1) * NG + 2)
                act.activation(rn[:, wide], rn[:, wide], ACT.Exp, scale=-0.5).then_inc(rn_ready, 1)

            with act.Fori(0, 3) as i:
                take(i, 0)
                silu(i, 0)
                take(i, 1)
                inverse_norm(i, 0)
                silu(i, 1)
                take(i, 2)
                inverse_norm(i, 1)
                silu(i, 2)

        @blk.gpsimd
        def _(pool):
            zero_pads(pool, (*raw, *con), pads)
            pool.memset(eps[:, 0:1], EPS * HD).then_inc(pads, 1)
            pool.memset(eps[:, 1:2], EPS).then_inc(pads, 1)
            pool.memset(rn[:], 0.0).then_inc(pads, 1)
            pool.wait_ge(pads, 6 * 3 + 2 + 1)
            with pool.Fori(0, 3) as i:
                for j in range(2):
                    pool.wait_ge(silu_ready, i * 3 + j + 1)
                    pool.tensor_tensor(con[j][:, wide], raw[j][:, wide], raw[j][:, wide], ALU.mult).then_inc(sq_ready, 1)

        @blk.vector
        def _(dve):
            dve.wait_ge(par_loaded, 32)
            dve.wait_ge(pads, 6 * 3 + 2 + 1)
            for i in range(3):
                s = Steps(dve, dve_own, i * DVE_OWN)

                def conv(j):
                    dve.wait_ge(row_ready, i * 3 + j + 1)
                    dve.wait_ge(stored[j], 16 * (i + 1))
                    out = con[j][:, wide]
                    s.link(dve.tensor_scalar(out, raw[j][:, OFF:OFF + CONV_N], taps[:, 3 * i + j, 0:1], None, ALU.mult))
                    for k in range(1, CW_B):
                        s.link(dve.scalar_tensor_tensor(out, raw[j][:, OFF + k:OFF + k + CONV_N], taps[:, 3 * i + j, k:k + 1],
                                                        out, ALU.mult, ALU.add))
                    dve.sem_inc(conv_ready, 1)

                def unit(j):
                    dve.wait_ge(rn_ready, 2 * i + j + 1)
                    s.link(dve.tensor_tensor(con[j][:, wide], raw[j][:, wide], rn[:, wide], ALU.mult))
                    dve.sem_inc(unit_ready, 1)

                conv(0)
                conv(1)
                unit(0)
                conv(2)
                unit(1)


def project_c(nc, t, lay, hT):
    with Mem(nc, f"pc{lay}") as m:
        w = [m.sb(f"w{b}", KT, P) for b in range(2)]
        row = [m.sb(f"row{b}", RL) for b in range(2)]
        acc = m.ps("acc", NG, 512)
        w_loaded, stored = m.sems("w_loaded", 2), m.sems("stored", 2)
        pads = m.sem("pads")
        acc_ready, acc_free, row_ready = m.sem("acc_ready"), m.sem("acc_free"), m.sem("row_ready")
        blk = m.block()
        n_s = NS - S_QC

        @blk.sync
        def _(sp):
            for b in range(2):
                sp.dma_start(w[b][:], t["w_in"][lay, S_QC + b]).then_inc(w_loaded[b], 16)
            with sp.Fori(0, n_s // 2) as i:
                for b in range(2):
                    s = i * 2 + b
                    sp.wait_ge(acc_ready, (s + 1) * NG)
                    sp.dma_start(w[b][:], t["w_in"][lay, ds1(s + S_QC + 2)].rearrange("a p k n -> p (a k) n")).then_inc(w_loaded[b], 16)
                    sp.wait_ge(row_ready, s + 1)
                    sp.dma_start(t["rows"][ds1(s + S_QC)].rearrange("a p n -> p (a n)"), row[b][:]).then_inc(stored[b], 16)
            for b in range(2):
                sp.wait_ge(stored[b], 16 * (n_s // 2 + 1))
                sp.wait_ge(w_loaded[b], 16 * (n_s // 2 + 1))

        @blk.tensor
        def _(pe):
            pe.sem_inc(acc_free, NG)
            with pe.Fori(0, n_s // 2) as i:
                for b in range(2):
                    pe.wait_ge(w_loaded[b], 16 * (i + 1))
                    project_slice(pe, i * 2 + b, w[b], hT, acc, acc_free, acc_ready)

        @blk.gpsimd
        def _(pool):
            zero_pads(pool, row, pads)

        @blk.scalar
        def _(act):
            for b in range(2):
                act.sem_inc(stored[b], 16)
            act.wait_ge(pads, 6)
            with act.Fori(0, n_s // 2) as i:
                for b in range(2):
                    act.wait_ge(stored[b], 16 * (i + 1))
                    take_out(act, i * 2 + b, acc, acc_ready, acc_free, row[b], ACT.Copy)
                    act.wait_ge(acc_free, (i * 2 + b + 2) * NG)
                    act.sem_inc(row_ready, 1)


def gates(nc, t, lay):
    G = 4 * NH
    with Mem(nc, f"gt{lay}") as m:
        sc = m.sb("sc", TOK)
        ident = m.sb("ident", P)
        dtb, alog, rate = m.sb("dtb", 2, NH), m.sb("alog", 2, NH), m.sb("rate", 2, NH)
        raw, out = m.sb("raw", NT, G), m.sb("out", NT, G)
        z, e, u, ln, pos, w, iszero = (m.sb(n, 2, NT, NH) for n in ("z", "e", "u", "ln", "pos", "w", "iszero"))
        tp = m.ps("tp", NT, G)
        loaded, turned, raw_ready = m.sem("loaded"), m.sem("turned"), m.sem("raw_ready")
        act_own, dve_own, stored = m.sem("act_own"), m.sem("dve_own"), m.sem("stored")
        blk = m.block()
        N_DVE = 2 + 4 + 6 + 2

        @blk.sync
        def _(sp):
            src = t["rows"][S_SC, 0:G]
            sp.dma_start(sc[0:G, 0:CTX], src[:, C0:C0 + CTX]).then_inc(loaded, 16)
            sp.dma_start(sc[0:G, CTX:TOK], src[:, L0:L0 + SEQ]).then_inc(loaded, 16)
            sp.dma_start(ident[:], t["ident"]).then_inc(loaded, 16)
            sp.dma_start(dtb[:], t["dt_bias"][lay]).then_inc(loaded, 16)
            sp.dma_start(alog[:], t["a_log"][lay]).then_inc(loaded, 16)
            sp.wait_ge(dve_own, N_DVE)
            sp.wait_ge(act_own, 6)
            sp.dma_start(t["gates"].rearrange("(t p) c -> p t c", p=P), out[:]).then_inc(stored, 16)
            sp.wait_ge(stored, 16)

        @blk.tensor
        def _(pe):
            pe.wait_ge(loaded, 5 * 16)
            for n in range(NT):
                mm = pe.transpose(tp[:, n, :], sc[0:G, n * P:(n + 1) * P], ident[0:G, 0:G])
            mm.then_inc(turned, 1)

        def part(x, d, kind):
            return x[:, :, (2 * d + kind) * NH:(2 * d + kind + 1) * NH]

        @blk.scalar
        def _(act):
            act.wait_ge(turned, 1)
            act.activation(raw[:], tp[:], ACT.Copy).then_inc(raw_ready, 1)
            s = Steps(act, act_own)
            s.link(act.activation(rate[:], alog[:], ACT.Exp))
            act.wait_ge(dve_own, 2)
            s.link(act.activation(e[:], z[:], ACT.Abs))
            s.link(act.activation(e[:], e[:], ACT.Exp, scale=-1.0))
            act.wait_ge(dve_own, 4)
            s.link(act.activation(ln[:], u[:], ACT.Ln))
            act.wait_ge(raw_ready, 1)
            for d in range(2):
                s.link(act.activation(part(out, d, 0), part(raw, d, 0), ACT.Sigmoid))

        @blk.vector
        def _(dve):
            dve.wait_ge(raw_ready, 1)
            s = Steps(dve, dve_own)
            for d in range(2):
                s.link(dve.tensor_tensor(z[:, d], part(raw, d, 1), dtb[:, d:d + 1, :].to_broadcast([P, NT, NH]), ALU.add))
            dve.wait_ge(act_own, 3)
            s.link(dve.tensor_scalar(u[:], e[:], 1.0, None, ALU.add))
            s.link(dve.tensor_scalar(pos[:], z[:], 0.0, None, ALU.max))
            s.link(dve.tensor_scalar(w[:], u[:], -1.0, None, ALU.add))
            s.link(dve.tensor_scalar(iszero[:], w[:], 0.0, None, ALU.is_equal))
            dve.wait_ge(act_own, 4)
            s.link(dve.tensor_tensor(w[:], w[:], iszero[:], ALU.add))
            s.link(dve.tensor_tensor(ln[:], ln[:], iszero[:], ALU.add))
            s.link(dve.reciprocal(w[:], w[:]))
            s.link(dve.tensor_tensor(e[:], e[:], w[:], ALU.mult))
            s.link(dve.tensor_tensor(e[:], e[:], ln[:], ALU.mult))
            s.link(dve.tensor_tensor(pos[:], pos[:], e[:], ALU.add))
            for d in range(2):
                s.link(dve.scalar_tensor_tensor(part(out, d, 1), pos[:, d], -1.0,
                                                rate[:, d:d + 1, :].to_broadcast([P, NT, NH]), ALU.mult, ALU.mult))
            assert s.n == N_DVE, s.n


def rotate(nc, t, lay):
    with Mem(nc, f"rot{lay}") as m:
        row = [m.sb(f"row{b}", RL) for b in range(2)]
        t1 = [m.sb(f"t1{b}", SEQ) for b in range(2)]
        t2 = [m.sb(f"t2{b}", SEQ) for b in range(2)]
        cos, sin = m.sb("cos", SEQ), m.sb("sin", SEQ)
        ident, swap = m.sb("ident", P), m.sb("swap", P)
        vrow, vt, zero = m.sb("vrow", RL), m.sb("vt", NT, P), m.sb("zero", P)
        ps = m.ps("ps", 4, 512)
        vps = m.ps("vps", 2, 512)
        row_loaded, stored = m.sems("row_loaded", 2), m.sems("stored", 2)
        par_loaded, v_loaded, zeroed, pad_stored = m.sem("par_loaded"), m.sem("v_loaded"), m.sem("zeroed"), m.sem("pad_stored")
        swapped, cos_done, sin_done, rotated = (m.sem(n) for n in ("swapped", "cos_done", "sin_done", "rotated"))
        v_turned, v_out, v_stored = m.sem("v_turned"), m.sem("v_out"), m.sem("v_stored")
        blk = m.block()
        lat = slice(L0, L0 + SEQ)
        NV = (NT + 3) // 4

        @blk.sync
        def _(sp):
            for n, dst in (("cos", cos), ("sin", sin), ("ident", ident), ("swap", swap)):
                sp.dma_start(dst[:], t[n]).then_inc(par_loaded, 16)
            sp.dma_start(vrow[:], t["rows"][S_VC]).then_inc(v_loaded, 16)
            for b in range(2):
                sp.sem_inc(stored[b], 32)
            with sp.Fori(0, 2) as i:
                for b in range(2):
                    sp.wait_ge(stored[b], 32 * (i + 1))
                    sp.dma_start(row[b][:], t["rows"][ds1(i * 2 + (S_QC + b))].rearrange("a p n -> p (a n)")).then_inc(row_loaded[b], 16)
                for b in range(2):
                    sp.wait_ge(rotated, 2 * i + b + 1)
                    for lo, n, col in ((0, CTX, C0), (CTX, SEQ, L0)):
                        sp.dma_start(t["qk"][ds1(i * 2 + b), :, lo:lo + n].rearrange("a p n -> p (a n)"), row[b][:, col:col + n]).then_inc(stored[b], 16)
            sp.wait_ge(zeroed, 1)
            sp.dma_start(t["qk"][3, :, TOK:TOK + KPAD], zero[:]).then_inc(pad_stored, 16)
            sp.dma_start(t["vt"][NT], zero[:]).then_inc(pad_stored, 16)
            sp.wait_ge(v_out, NV)
            sp.dma_start(t["vt"][0:NT].rearrange("t p c -> p t c"), vt[:]).then_inc(v_stored, 16)
            sp.wait_ge(v_stored, 16)
            sp.wait_ge(pad_stored, 32)
            for b in range(2):
                sp.wait_ge(stored[b], 32 * 3)

        @blk.tensor
        def _(pe):
            pe.wait_ge(par_loaded, 4 * 16)
            pe.sem_inc(sin_done, 4)
            with pe.Fori(0, 2) as i:
                for b in range(2):
                    pe.wait_ge(row_loaded[b], 16 * (i + 1))
                    for g in range(4):
                        pe.wait_ge(sin_done, (2 * i + b) * 4 + g + 1)
                        pe.matmul(ps[:, g, :], swap[:], row[b][:, L0 + 512 * g:L0 + 512 * g + 512], start=True, stop=True).then_inc(swapped, 1)
            pe.wait_ge(v_loaded, 16)
            for q in range(NV):
                if q >= 2:
                    pe.wait_ge(v_out, q - 1)
                for n in range(4 * q, min(4 * q + 4, NT)):
                    col = C0 + n * P if n < NCT else L0 + (n - NCT) * P
                    mm = pe.transpose(vps[:, q % 2, (n % 4) * P:(n % 4 + 1) * P], vrow[:, col:col + P], ident[:])
                mm.then_inc(v_turned, 1)

        @blk.scalar
        def _(act):
            for q in range(NV):
                n = min(4, NT - 4 * q)
                act.wait_ge(v_turned, q + 1)
                act.activation(vt[:, 4 * q:4 * q + n, :], vps[:, q % 2, 0:n * P].rearrange("p (t c) -> p t c", c=P), ACT.Copy).then_inc(v_out, 1)

        @blk.gpsimd
        def _(pool):
            pool.memset(zero[:], 0.0).then_inc(zeroed, 1)
            pool.wait_ge(par_loaded, 4 * 16)
            with pool.Fori(0, 2) as i:
                for b in range(2):
                    pool.wait_ge(row_loaded[b], 16 * (i + 1))
                    pool.wait_ge(rotated, 2 * i)
                    pool.tensor_tensor(t1[b][:], row[b][:, lat], cos[:], ALU.mult).then_inc(cos_done, 1)

        @blk.vector
        def _(dve):
            dve.wait_ge(par_loaded, 4 * 16)
            with dve.Fori(0, 2) as i:
                for b in range(2):
                    for g in range(4):
                        dve.wait_ge(swapped, (2 * i + b) * 4 + g + 1)
                        dve.tensor_tensor(t2[b][:, 512 * g:512 * g + 512], ps[:, g, :], sin[:, 512 * g:512 * g + 512], ALU.mult).then_inc(sin_done, 1)
                    dve.wait_ge(sin_done, (2 * i + b + 2) * 4)
                    dve.wait_ge(cos_done, 2 * i + b + 1)
                    dve.tensor_tensor(row[b][:, lat], t1[b][:], t2[b][:], ALU.add).then_inc(rotated, 1)


def attention(nc, t, lay, ctx):
    nk = NCT if ctx else NCT + 3
    half = nk * P // 2
    n_q = NCT if ctx else SEQ // P
    SC = float(HD) ** -0.5
    with Mem(nc, f"at{lay}{int(ctx)}") as m:
        ident = m.sb("ident", P)
        sink, sink_raw = m.sb("sink", NH), m.sb("sink_raw", NH)
        q = [m.sb(f"q{b}", 3, P) for b in range(2)]
        k = [m.sb(f"k{b}", nk * P) for b in range(2)]
        v = [m.sb(f"v{b}", nk, P) for b in range(2)]
        mask = [m.sb(f"mask{b}", 2 * P) for b in range(2)]
        z = [m.sb(f"z{b}", 3, P) for b in range(2)]
        y = [m.sb(f"y{b}", 3, P) for b in range(2)]
        p = [m.sb(f"p{b}", nk * P) for b in range(2)]
        pt = [m.sb(f"pt{b}", nk, 3, P) for b in range(2)]
        mx, nb, l, es = (m.sb(n, NH) for n in ("mx", "nb", "l", "es"))
        sps = m.ps("sps", 2, 2, 512)
        tps = m.ps("tps", 2, 512)
        ops = m.ps("ops", 2, 512)
        par_loaded, sink_ready = m.sem("par_loaded"), m.sem("sink_ready")
        loaded, stored = m.sems("loaded", 2), m.sems("stored", 2)
        s_ready, nb_ready, exp_done, p_ready = (m.sem(n) for n in ("s_ready", "nb_ready", "exp_done", "p_ready"))
        t_ready, t_act, t_dve, o_ready, y_ready = (m.sem(n) for n in ("t_ready", "t_act", "t_dve", "o_ready", "y_ready"))
        dve_own, es_done = m.sem("dve_own"), m.sem("es_done")
        blk = m.block()
        n_load = 2 if ctx else 9
        split = (nk + 1) // 2

        @blk.sync
        def _(sp):
            sp.dma_start(ident[:], t["ident"]).then_inc(par_loaded, 16)
            sp.dma_start(sink_raw[:], t["sink"][lay]).then_inc(par_loaded, 16)
            for b in range(2):
                sp.sem_inc(stored[b], 16)
                sp.dma_start(k[b][:, (nk - NCT) * P:], t["qk"][3, :, 0:CTX]).then_inc(par_loaded, 16)
                sp.dma_start(v[b][:, nk - NCT:, :], t["vt"][0:NCT].rearrange("t p c -> p t c")).then_inc(par_loaded, 16)
            sp.sem_inc(o_ready, 4)
            sp.sem_inc(y_ready, 4)
            with sp.Fori(0, n_q // 2) as i:
                for b in range(2):
                    n = i * 2 + b
                    sp.wait_ge(o_ready, 2 * n + 2)
                    sp.wait_ge(y_ready, 2 * n + 2)
                    tok = n * P + (0 if ctx else CTX)
                    col = n * P + (C0 if ctx else L0)
                    sp.dma_start(q[b][:], t["qk"][0:3, :, bass.ds(tok, P)].rearrange("j p n -> p j n")).then_inc(loaded[b], 16)
                    sp.dma_start(z[b][:], t["rows"][9:12, :, bass.ds(col, P)].rearrange("j p n -> p j n")).then_inc(loaded[b], 16)
                    if not ctx:
                        for a, off in enumerate((-1, 1, 0)):
                            sp.dma_start(k[b][:, a * P:(a + 1) * P], t["qk"][3, :, bass.ds(n * P + (CTX + off * P), P)]).then_inc(loaded[b], 16)
                            sp.dma_start(v[b][:, a:a + 1, :], t["vt"][ds1(n + (NCT + off))].rearrange("t p c -> p t c")).then_inc(loaded[b], 16)
                        sp.dma_start(mask[b][:], t["mask"][ds1(n)].rearrange("t p c -> p (t c)")).then_inc(loaded[b], 16)
                for b in range(2):
                    n = i * 2 + b
                    sp.wait_ge(y_ready, 2 * n + 6)
                    tok = n * P + (0 if ctx else CTX)
                    sp.dma_start(t["yc"][:, :, bass.ds(tok, P)].rearrange("j p n -> p j n"), y[b][:]).then_inc(stored[b], 16)
            for b in range(2):
                sp.wait_ge(stored[b], 16 * (n_q // 2 + 1))

        @blk.tensor
        def _(pe):
            pe.wait_ge(par_loaded, 6 * 16)
            pe.sem_inc(exp_done, 2)
            pe.sem_inc(t_act, 1)
            pe.sem_inc(t_dve, 1)

            def scores(n, b, u):
                g, j = divmod(u, 3)
                pe.wait_ge(exp_done, n * NH + u + 1)
                for h in range(2):
                    mm = pe.matmul(sps[:, u % 2, h, 0:half], q[b][g * HD:(g + 1) * HD, j, :],
                                   k[b][g * HD:(g + 1) * HD, h * half:(h + 1) * half], start=True, stop=True)
                mm.then_inc(s_ready, 1)

            def turn(n, u):
                pe.wait_ge(p_ready, n * NH + u + 1)
                pe.wait_ge(t_act, n * NH + u + 1)
                pe.wait_ge(t_dve, n * NH + u + 1)
                for a in range(nk):
                    h, c = (0, a) if a < split else (1, a - split)
                    mm = pe.transpose(tps[:, h, c * P:(c + 1) * P], p[u % 2][:, a * P:(a + 1) * P], ident[:])
                mm.then_inc(t_ready, 1)

            def values(n, b, g):
                pe.wait_ge(t_act, n * NH + 3 * g + 4)
                pe.wait_ge(t_dve, n * NH + 3 * g + 4)
                pe.wait_ge(y_ready, 2 * n + g + 1)
                for a in range(nk):
                    mm = pe.matmul(ops[g * HD:(g + 1) * HD, b, 0:3 * P], v[b][:, a, g * HD:(g + 1) * HD],
                                   pt[g][:, a, :, :].rearrange("p j n -> p (j n)"), start=(a == 0), stop=(a == nk - 1))
                mm.then_inc(o_ready, 1)

            with pe.Fori(0, n_q // 2) as i:
                for b in range(2):
                    n = i * 2 + b
                    pe.wait_ge(loaded[b], 16 * n_load * (i + 1))
                    scores(n, b, 0)
                    scores(n, b, 1)
                    for u in range(NH):
                        turn(n, u)
                        if u + 2 < NH:
                            scores(n, b, u + 2)
                        if u == 3:
                            values(n, b, 0)
                    values(n, b, 1)

        @blk.scalar
        def _(act):
            def exps(n, u):
                act.wait_ge(nb_ready, n * NH + u + 1)
                act.wait_ge(t_ready, n * NH + u - 1) if u >= 2 else act.wait_ge(t_ready, n * NH)
                act.activation(p[u % 2][:].rearrange("p (h c) -> p h c", h=2), sps[:, u % 2, :, 0:half], ACT.Exp, scale=SC, bias=nb[:, u:u + 1],
                               accum_out=l[:, u:u + 1]).then_inc(exp_done, 1)
                act.activation(es[:, u:u + 1], sink_raw[:, u:u + 1], ACT.Exp, bias=nb[:, u:u + 1]).then_inc(es_done, 1)

            def move(n, u):
                g, j = divmod(u, 3)
                act.wait_ge(t_ready, n * NH + u + 1)
                if j == 0:
                    act.wait_ge(o_ready, 2 * n + g + 3)
                act.activation(pt[g][:, 0:split, j, :], tps[:, 0, 0:split * P].rearrange("p (a n) -> p a n", a=split), ACT.Copy).then_inc(t_act, 1)

            act.wait_ge(par_loaded, 6 * 16)
            with act.Fori(0, n_q // 2) as i:
                for b in range(2):
                    n = i * 2 + b
                    exps(n, 0)
                    for u in range(NH):
                        if u + 1 < NH:
                            exps(n, u + 1)
                        move(n, u)

        N_OWN = (4 if ctx else 5) * NH

        @blk.vector
        def _(dve):
            dve.wait_ge(par_loaded, 6 * 16)
            dve.tensor_scalar(sink[:], sink_raw[:], 1.0 / SC, None, ALU.mult).then_inc(sink_ready, 1)
            dve.wait_ge(sink_ready, 1)

            def highest(s, n, b, u):
                dve.wait_ge(s_ready, n * NH + u + 1)
                if not ctx:
                    s.link(dve.tensor_tensor(sps[:, u % 2, 0, 0:2 * P], sps[:, u % 2, 0, 0:2 * P], mask[b][:], ALU.add))
                s.link(dve.tensor_reduce(mx[:, u:u + 1], sps[:, u % 2, :, 0:half], AX.XY, ALU.max))
                dve.tensor_scalar(nb[:, u:u + 1], mx[:, u:u + 1], sink[:, u:u + 1], -SC, ALU.max, ALU.mult).then_inc(nb_ready, 1)

            def weigh(s, n, u):
                dve.wait_ge(exp_done, n * NH + u + 3)
                dve.wait_ge(es_done, n * NH + u + 1)
                s.link(dve.tensor_tensor(l[:, u:u + 1], l[:, u:u + 1], es[:, u:u + 1], ALU.add))
                s.link(dve.reciprocal(l[:, u:u + 1], l[:, u:u + 1]))
                s.inc(dve.tensor_scalar(p[u % 2][:], p[u % 2][:], l[:, u:u + 1], None, ALU.mult))
                dve.wait_ge(s.sem, s.at + s.n)
                dve.sem_inc(p_ready, 1)

            def move(n, u):
                g, j = divmod(u, 3)
                dve.wait_ge(t_ready, n * NH + u + 1)
                if j == 0:
                    dve.wait_ge(o_ready, 2 * n + g + 3)
                dve.tensor_copy(pt[g][:, split:nk, j, :], tps[:, 1, 0:(nk - split) * P].rearrange("p (a n) -> p a n", a=nk - split)).then_inc(t_dve, 1)

            def gated(n, b, g):
                dve.wait_ge(o_ready, 2 * n + g + 5)
                h = slice(g * HD, (g + 1) * HD)
                dve.tensor_tensor(y[b][h], ops[h, b, 0:3 * P].rearrange("p (j n) -> p j n", j=3), z[b][h], ALU.mult).then_inc(y_ready, 1)

            with dve.Fori(0, n_q // 2) as i:
                for b in range(2):
                    n = i * 2 + b
                    s = Steps(dve, dve_own, n * N_OWN)
                    dve.wait_ge(loaded[b], 16 * n_load * (i + 1))
                    dve.wait_ge(stored[b], 16 * (i + 1))
                    highest(s, n, b, 0)
                    for u in range(NH):
                        if u + 1 < NH:
                            highest(s, n, b, u + 1)
                        weigh(s, n, u)
                        move(n, u)
                        if u == 4:
                            gated(n, b, 0)
                    gated(n, b, 1)
                    assert s.n == N_OWN, s.n


def deltanet(nc, t, lay):
    H = [(h, h // 2, h % 2) for h in range(NH)]
    LEVELS = [2, 4, 8, 16, 32]
    NL = len(LEVELS) + 1
    with Mem(nc, f"dn{lay}") as m:
        ident, blockdiag, tri = m.sb("ident", P), m.sb("blockdiag", P), m.sb("tri", P)
        tri_c, negmask, eye_c = m.sb("tri_c", CH), m.sb("negmask", CH), m.sb("eye_c", CH)
        lmask, umask1 = m.sb("lmask", NL, CH), m.sb("umask1", CH)
        dirmask, ones = m.sb("dirmask", 2), m.sb("ones", HD)
        kq = [m.sb(f"kq{b}", NP3, 2, 2, CH) for b in range(2)]
        vf = [m.sb(f"vf{b}", NP3, 2, CH) for b in range(2)]
        gb = [m.sb(f"gb{b}", 2, NH) for b in range(2)]
        gtri = m.sb("gtri", NH, CH)
        gz = m.sb("gz", 2, NP3, 2)
        expo = m.sb("expo", 3, NH)
        ex = [m.sb(f"ex{b}", 3, NH) for b in range(2)]
        bw = [m.sb(f"bw{b}", NH) for b in range(2)]
        xm, dec_in, dec, decb = (m.sb(n, NH, CH) for n in ("xm", "dec_in", "dec", "decb"))
        n_t, tmp = m.sb("n_t", NH, CH), m.sb("tmp", NH, CH)
        at = [m.sb(f"at{b}", NH, CH) for b in range(2)]
        kt = [m.sb(f"kt{b}", NH, CH) for b in range(2)]
        vt = [m.sb(f"vt{b}", NH, CH) for b in range(2)]
        T, M = m.sb("T", NH, CH), m.sb("M", NH, CH)
        TT = [m.sb(f"TT{b}", NH, CH) for b in range(2)]
        state, faded = m.sb("state", NP3, 2, CH), m.sb("faded", NP3, 2, CH)
        kqs = m.sb("kqs", NH, 2, CH)
        rest, v_new, v_dec = m.sb("rest", NH, CH), m.sb("v_new", NH, CH), m.sb("v_dec", NH, CH)
        o = [m.sb(f"o{b}", NH, CH) for b in range(2)]
        p_kq = m.ps("p_kq", 2, 512)
        p_g, p_k, p_v = m.ps("p_g", 512), m.ps("p_k", 512), m.ps("p_v", 512)
        l_m, l_t, l_tt = m.ps("l_m", 512), m.ps("l_t", 512), m.ps("l_tt", 512)

        par_loaded, loaded = m.sem("par_loaded"), m.sems("loaded", 2)
        gates_ready, sums_done, grow_done, kv_done, kq_done = (m.sem(n) for n in ("gates_ready", "sums_done", "grow_done", "kv_done", "kq_done"))
        sums_out, expo_ready, ex_ready, bw_ready = (m.sem(n) for n in ("sums_out", "expo_ready", "ex_ready", "bw_ready"))
        xm_ready, dvec_ready, dec_ready, decb_ready = (m.sem(n) for n in ("xm_ready", "dvec_ready", "dec_ready", "decb_ready"))
        kv_out, nt_ready, at_ready, tt0_ready, pool_own = (m.sem(n) for n in ("kv_out", "nt_ready", "at_ready", "tt0_ready", "pool_own"))
        lm_done, m_ready, lt_done, t_ready, tt_ready = (m.sem(n) for n in ("lm_done", "m_ready", "lt_done", "t_ready", "tt_ready"))
        ks_done, kqs_ready, rest_ready, tr_done, vn_ready = (m.sem(n) for n in ("ks_done", "kqs_ready", "rest_ready", "tr_done", "vn_ready"))
        av_done, faded_ready, state_ready, o_ready = (m.sem(n) for n in ("av_done", "faded_ready", "state_ready", "o_ready"))
        o_stored, waits_passed = m.sems("o_stored", 2), m.sem("waits_passed")
        blk = m.block()

        def wait_apart(pe, sem, value):
            pe.wait_ge(sem, value)
            pe.sem_inc(waits_passed, 1)

        def heads(bank):
            return bank[:, 0:NH * CH].rearrange("p (h c) -> p h c", h=NH)

        def col(h):
            return slice(h * CH, (h + 1) * CH)

        DIRS = [(d, slice(d * CH, (d + 1) * CH)) for d in range(2)]
        HALF = [slice(0, HD), slice(HD, P)]

        def per_head(x):
            return x.unsqueeze(2).to_broadcast([P, NH, CH])

        def all_heads(x):
            return x.unsqueeze(1).to_broadcast([P, NH, CH])

        N_LOAD = 8

        @blk.sync
        def _(sp):
            for dst, n in ((ident, "ident"), (blockdiag, "blockdiag"), (tri, "tri"), (tri_c, "tri_c"), (negmask, "negmask"),
                           (eye_c, "eye_c"), (lmask, "lmask"), (umask1, "umask1"), (dirmask, "dirmask"), (ones, "ones")):
                sp.dma_start(dst[:], t[n]).then_inc(par_loaded, 16)

            def load(b, fcol, bcol, ftok, btok):
                for d, (c, tok) in enumerate(((fcol, ftok), (bcol, btok))):
                    for kind in range(3):
                        src = t["rows"][S_QKV + kind:S_QKV + 9:3, :, bass.ds(c, CH)].rearrange("s p c -> p s c")
                        dst = vf[b][:, :, d, :] if kind == 2 else kq[b][:, :, 1 - kind, d, :]
                        sp.dma_start(dst, src).then_inc(loaded[b], 16)
                    sp.dma_start(gb[b][d * CH:(d + 1) * CH], t["gates"][bass.ds(tok, CH), d * 2 * NH:(d + 1) * 2 * NH]
                                 .rearrange("p (k h) -> p k h", k=2)).then_inc(loaded[b], 16)

            def store(n, b, ftok, btok):
                sp.wait_ge(o_ready, n + 1)
                for (d, part), tok in zip(DIRS, (ftok, btok)):
                    sp.dma_start(t["scan"][d, bass.ds(tok, CH), :], o[b][part].rearrange("p h c -> p (h c)")).then_inc(o_stored[b], 16)

            def turn(i, b, fcol, bcol, ftok, btok, prev):
                n = i * 2 + b
                sp.wait_ge(state_ready, n)
                load(b, fcol, bcol, ftok, btok)
                if prev is not None:
                    store(n - 1, 1 - b, *prev)

            def ctx_at(n):
                return (n * CH + C0, (NCSTEP - 1 - n) * CH + C0, n * CH, (NCSTEP - 1 - n) * CH)

            def lat_at(n):
                last = NSTEP + NCSTEP - 1
                return (n * CH + (L0 - CTX), n * -CH + (last * CH + L0 - CTX), n * CH, n * -CH + last * CH)

            for n in range(NCSTEP):
                turn(n // 2, n % 2, *ctx_at(n), None if n == 0 else ctx_at(n - 1)[2:])
            for b in range(2):
                n = NCSTEP + b
                turn(n // 2, b, *lat_at(n), (ctx_at(n - 1) if b == 0 else lat_at(n - 1))[2:])
            with sp.Fori(NCSTEP // 2 + 1, NSTEP // 2) as i:
                for b in range(2):
                    turn(i, b, *lat_at(i * 2 + b), lat_at(i * 2 + (b - 1))[2:])
            store(NSTEP - 1, 1, *lat_at(NSTEP - 1)[2:])
            for b in range(2):
                sp.wait_ge(o_stored[b], 32 * (NSTEP // 2))

        @blk.tensor
        def _(pe):
            pe.wait_ge(par_loaded, 10 * 16)

            def prepare(n, b, i):
                pe.wait_ge(loaded[b], 16 * N_LOAD * (i + 1))
                pe.wait_ge(kv_out, n)
                pe.wait_ge(at_ready, n)
                pe.wait_ge(state_ready, n)
                if not (isinstance(n, int) and n == 0):
                    pe.wait_ge(o_ready, n - 1)
                for pair in range(NP3):
                    pe.transpose(p_k[:, pair * P:(pair + 1) * P], kq[b][:, pair, 0].rearrange("p d c -> p (d c)"), ident[:])
                for pair in range(NP3):
                    mm = pe.transpose(p_v[:, pair * P:(pair + 1) * P], vf[b][:, pair].rearrange("p d c -> p (d c)"), ident[:])
                mm.then_inc(kv_done, 1)
                for h, pair, hh in H:
                    for d, part in DIRS:
                        mm = pe.matmul(p_kq[part, hh, pair * P:(pair + 1) * P], kq[b][HALF[hh], pair, 0, d, :],
                                       kq[b][HALF[hh], pair, :, d, :], start=True, stop=True)
                mm.then_inc(kq_done, 1)
                pe.wait_ge(gates_ready, n + 1)
                g = gb[b][:, 1, :]
                pe.matmul(p_g[:, 384:390], tri[:], g, start=True, stop=True)
                pe.matmul(p_g[:, 390:396], blockdiag[:], g, start=True, stop=True)
                for hh in range(2):
                    pe.matmul(p_g[HALF[hh], 396:402], ones[:], gz[:, hh].rearrange("p a d -> p (a d)"), start=True, stop=True)
                pe.matmul(p_g[:, 0:384], blockdiag[:], gtri[:].rearrange("p h c -> p (h c)"), start=True, stop=True).then_inc(grow_done, 1)

            def square(bank, lhs, rhs):
                for h in range(NH):
                    for d, part in DIRS:
                        mm = pe.matmul(bank[part, col(h)], lhs[part, h, :], rhs[part, h, :], start=True, stop=True)
                return mm

            def body(n, b, scan, i=None):
                i = n // 2 if isinstance(n, int) else i
                prepare(n, b, i)
                B = 1 - b
                wait_apart(pe, nt_ready, n + 1)
                for h in range(NH):
                    for d, part in DIRS:
                        mm = pe.matmul(l_m[part, col(h)], n_t[part, h, :], eye_c[part], start=True, stop=True)
                mm.then_inc(lm_done, 1)
                if scan:
                    pe.wait_ge(at_ready, n + 1)
                    wait_apart(pe, state_ready, n)
                    s_products(B)
                for lv in range(len(LEVELS)):
                    q = n * NL + lv
                    pe.wait_ge(t_ready, n * (NL - 1) + lv + 1)
                    wait_apart(pe, tt_ready, q + 1)
                    square(l_m, n_t, T).then_inc(lm_done, 1)
                    if scan and lv == 0:
                        pe.wait_ge(rest_ready, n)
                        wait_apart(pe, dvec_ready, n + 1)
                        square(p_g, TT[B], rest).then_inc(tr_done, 1)
                    if scan and lv == 2:
                        pe.wait_ge(vn_ready, n)
                        wait_apart(pe, kv_out, n + 1)
                        v_products(B)
                    wait_apart(pe, m_ready, q + 2)
                    if lv + 1 < len(LEVELS):
                        square(l_t, TT[b], M)
                    square(l_tt, M, TT[b]).then_inc(lt_done, 1)

            def s_products(B):
                for h, pair, hh in H:
                    for d, part in DIRS:
                        for k in range(2):
                            mm = pe.matmul(p_kq[part, hh, pair * P + k * CH:pair * P + (k + 1) * CH], kq[B][HALF[hh], pair, k, d, :],
                                           state[HALF[hh], pair, d, :], start=True, stop=True)
                mm.then_inc(ks_done, 1)

            def v_products(B):
                square(p_k, at[B], v_new)
                for h, pair, hh in H:
                    for d, part in DIRS:
                        mm = pe.matmul((p_v, p_g)[d][HALF[hh], pair * CH:(pair + 1) * CH], kt[B][part, h, :], v_dec[part, h, :], start=True, stop=True)
                mm.then_inc(av_done, 1)

            def tail(n, b):
                pe.wait_ge(tt_ready, (n + 1) * NL)
                pe.wait_ge(state_ready, n + 1)
                s_products(b)
                pe.wait_ge(rest_ready, n + 1)
                square(p_g, TT[b], rest).then_inc(tr_done, 1)
                pe.wait_ge(vn_ready, n + 1)
                v_products(b)

            body(0, 0, False)
            body(1, 1, True)
            with pe.Fori(1, NSTEP // 2) as i:
                for b in range(2):
                    body(i * 2 + b, b, True, i)
            tail(NSTEP - 1, 1)

        @blk.scalar
        def _(act):
            act.wait_ge(par_loaded, 10 * 16)

            def body(n, b):
                act.wait_ge(grow_done, n + 1)
                act.wait_ge(bw_ready, n)
                act.activation(expo[:], p_g[:, 384:402].rearrange("p (k h) -> p k h", k=3), ACT.Copy).then_inc(sums_out, 1)
                act.wait_ge(expo_ready, n + 1)
                act.activation(ex[b][:], expo[:], ACT.Exp).then_inc(ex_ready, 1)
                act.wait_ge(dvec_ready, n + 1)
                act.wait_ge(at_ready, n)
                act.activation(dec[:], dec_in[:], ACT.Exp).then_inc(dec_ready, 1)
                act.wait_ge(kv_done, n + 1)
                act.activation(kt[b][:], heads(p_k), ACT.Copy)
                act.activation(vt[b][:], heads(p_v), ACT.Copy).then_inc(kv_out, 1)

            with act.Fori(0, NSTEP // 2) as i:
                for b in range(2):
                    body(i * 2 + b, b)

        @blk.gpsimd
        def _(pool):
            pool.wait_ge(par_loaded, 10 * 16)

            def body(n, b, scan, i=None):
                i = n // 2 if isinstance(n, int) else i
                pool.wait_ge(loaded[b], 16 * N_LOAD * (i + 1))
                pool.wait_ge(grow_done, n)
                g, beta = gb[b][:, 1, :], gb[b][:, 0, :]
                pool.tensor_tensor(gtri[:], all_heads(tri_c[:]), per_head(g), ALU.mult)
                g4 = g.rearrange("p (a h) -> p h a", h=2)
                for hh in range(2):
                    ins = pool.tensor_tensor(gz[:, hh], g4[:, hh, :].unsqueeze(2).to_broadcast([P, NP3, 2]),
                                             dirmask[:].unsqueeze(1).to_broadcast([P, NP3, 2]), ALU.mult)
                ins.then_inc(gates_ready, 1)
                if scan:
                    pool.wait_ge(state_ready, n)
                    pool.tensor_tensor(faded[:].rearrange("p a d c -> p (a d) c"), state[:].rearrange("p a d c -> p (a d) c"),
                                       per_head(ex[1 - b][:, 2, :]), ALU.mult).then_inc(faded_ready, 1)
                pool.wait_ge(sums_out, n + 1)
                pool.wait_ge(dvec_ready, n)
                pool.tensor_tensor(xm[:], all_heads(negmask[:]), per_head(expo[:, 0, :]), ALU.subtract).then_inc(xm_ready, 1)
                pool.tensor_tensor(expo[:, 1, :], expo[:, 1, :], expo[:, 0, :], ALU.subtract).then_inc(expo_ready, 1)
                pool.wait_ge(ex_ready, n + 1)
                pool.tensor_tensor(bw[b][:], beta, ex[b][:, 1, :], ALU.mult).then_inc(bw_ready, 1)
                pool.wait_ge(dec_ready, n + 1)
                pool.tensor_tensor(decb[:], dec[:], per_head(beta), ALU.mult).then_inc(decb_ready, 1)
                pool.wait_ge(nt_ready, n + 1)
                pool.tensor_tensor(tmp[:], n_t[:], all_heads(umask1[:]), ALU.mult).then_inc(pool_own, 1)
                pool.wait_ge(pool_own, n + 1)
                pool.tensor_tensor(TT[b][:], all_heads(eye_c[:]), tmp[:], ALU.subtract).then_inc(tt_ready, 1)

            body(0, 0, False)
            body(1, 1, True)
            with pool.Fori(1, NSTEP // 2) as i:
                for b in range(2):
                    body(i * 2 + b, b, True, i)
            pool.wait_ge(state_ready, NSTEP)
            pool.tensor_tensor(faded[:].rearrange("p a d c -> p (a d) c"), state[:].rearrange("p a d c -> p (a d) c"),
                               per_head(ex[1][:, 2, :]), ALU.mult).then_inc(faded_ready, 1)

        @blk.vector
        def _(dve):
            dve.memset(state[:], 0.0).then_inc(state_ready, 1)
            dve.wait_ge(par_loaded, 10 * 16)

            def kq_bank(k):
                return p_kq[:, :, 0:3 * P].rearrange("p h (a k c) -> p h a k c", a=NP3, k=2)[:, :, :, k, :]

            def split(x):
                return x.rearrange("p (a h) c -> p h a c", h=2)

            def body(n, b, scan, i=None):
                i = n // 2 if isinstance(n, int) else i
                dve.wait_ge(xm_ready, n + 1)
                dve.tensor_tensor(dec_in[:], heads(p_g), xm[:], ALU.add).then_inc(dvec_ready, 1)
                dve.wait_ge(kq_done, n + 1)
                dve.wait_ge(decb_ready, n + 1)
                dve.wait_ge(tt_ready, n * NL)
                dve.tensor_tensor(split(n_t[:]), kq_bank(0), split(decb[:]), ALU.mult).then_inc(nt_ready, 1)
                dve.tensor_tensor(split(at[b][:]), kq_bank(1), split(dec[:]), ALU.mult).then_inc(at_ready, 1)
                for lv in range(NL):
                    q = n * NL + lv
                    dve.wait_ge(lm_done, q + 1)
                    dve.tensor_tensor(M[:], heads(l_m), all_heads(lmask[:, lv, :]), ALU.mult).then_inc(m_ready, 1)
                    if lv == 0:
                        dve.wait_ge(m_ready, q + 1)
                        dve.tensor_tensor(T[:], all_heads(eye_c[:]), M[:], ALU.subtract).then_inc(t_ready, 1)
                        if scan:
                            dve.wait_ge(ks_done, n)
                            scan_front(n - 1, 1 - b)
                    else:
                        if scan and lv == 1:
                            scan_values(n - 1, 1 - b)
                        if scan and lv == 3:
                            scan_end(n - 1, 1 - b, i - 1 + b)
                        dve.wait_ge(lt_done, n * (NL - 1) + lv)
                        if lv + 1 < NL:
                            dve.tensor_tensor(T[:], T[:], heads(l_t), ALU.subtract).then_inc(t_ready, 1)
                        dve.tensor_tensor(TT[b][:], TT[b][:], heads(l_tt), ALU.subtract).then_inc(tt_ready, 1)

            def scan_front(s, b):
                for hh in range(2):
                    ins = dve.tensor_tensor(kqs[:].rearrange("p (a h) k c -> p h a (k c)", h=2)[:, hh],
                                            p_kq[:, hh, 0:NP3 * P].rearrange("p (a c) -> p a c", a=NP3),
                                            ex[b][:, 0, :].rearrange("p (a h) -> p h a", h=2)[:, hh].unsqueeze(2).to_broadcast([P, NP3, P]),
                                            ALU.mult)
                ins.then_inc(kqs_ready, 1)
                dve.wait_ge(kqs_ready, s + 1)
                dve.tensor_tensor(rest[:], vt[b][:], kqs[:, :, 0, :], ALU.subtract).then_inc(rest_ready, 1)

            def scan_values(s, b):
                dve.wait_ge(tr_done, s + 1)
                dve.tensor_tensor(v_new[:], heads(p_g), per_head(gb[b][:, 0, :]), ALU.mult)
                dve.tensor_tensor(v_dec[:], heads(p_g), per_head(bw[b][:]), ALU.mult).then_inc(vn_ready, 1)

            def scan_end(s, b, before):
                dve.wait_ge(av_done, s + 1)
                dve.wait_ge(faded_ready, s + 1)
                dve.wait_ge(o_stored[b], before * 32)
                dve.tensor_tensor(o[b][:], kqs[:, :, 1, :], heads(p_k), ALU.add).then_inc(o_ready, 1)
                for d, bank in enumerate((p_v, p_g)):
                    ins = dve.tensor_tensor(state[:, :, d, :], faded[:, :, d, :], bank[:, 0:NP3 * CH].rearrange("p (a c) -> p a c", a=NP3), ALU.add)
                ins.then_inc(state_ready, 1)

            def tail(s, b):
                dve.wait_ge(ks_done, s + 1)
                scan_front(s, b)
                scan_values(s, b)
                scan_end(s, b, NSTEP // 2 - 1)

            body(0, 0, False)
            body(1, 1, True)
            with dve.Fori(1, NSTEP // 2) as i:
                for b in range(2):
                    body(i * 2 + b, b, True, i)
            tail(NSTEP - 1, 1)


def finish(nc, t, lay):
    last = lay == DEPTH - 1
    first = NCT if last else 0
    n_t = NT - first
    with Mem(nc, f"fin{lay}") as m:
        ident, mean_w = m.sb("ident", P), m.sb("mean_w", P)
        w = m.sb("w", KT, D)
        gate = m.sb("gate", 2, D)
        fnw, ln_w, ln_b, dn_w, eps = m.sb("fnw", D), m.sb("ln_w", 2), m.sb("ln_b", 2), m.sb("dn_w", 1), m.sb("eps", 1)
        u = [m.sb(f"u{b}", 2, P) for b in range(2)]
        za = [m.sb(f"za{b}", 2, P) for b in range(2)]
        zb = [m.sb(f"zb{b}", 3, P) for b in range(2)]
        of = [m.sb(f"of{b}", NH, HD) for b in range(2)]
        ob = [m.sb(f"ob{b}", NH, HD) for b in range(2)]
        x = [m.sb(f"x{b}", D) for b in range(2)]
        y = [m.sb(f"y{b}", KT, P) for b in range(2)]
        usq, rs, osq = m.sb("usq", 2, P), m.sb("rs", P), m.sb("osq", NH, HD)
        oss, orn = m.sb("oss", NH), m.sb("orn", NH)
        gy = m.sb("gy", D)
        xo = [m.sb(f"xo{b}", D) for b in range(2)]
        xss, sq = m.sb("xss", 1), m.sb("sq", D)
        res = [m.sb(f"res{b}", D) for b in range(2)]
        mps = m.ps("mps", 2, 512)
        tps = m.ps("tps", 512)
        ops = m.ps("ops", 2, 2, 512)
        par_loaded, eps_ready = m.sem("par_loaded"), m.sem("eps_ready")
        loaded, stored = m.sems("loaded", 2), m.sems("stored", 2)
        mean_done, var_done, turned, out_done = (m.sem(n) for n in ("mean_done", "var_done", "turned", "out_done"))
        centred, usq_ready, rs_ready, un_ready, silu_ready, ya_ready = (m.sem(n) for n in ("centred", "usq_ready", "rs_ready", "un_ready", "silu_ready", "ya_ready"))
        o_ready, osq_ready, oss_ready, orn_ready, on_ready, yb_ready = (m.sem(n) for n in ("o_ready", "osq_ready", "oss_ready", "orn_ready", "on_ready", "yb_ready"))
        gy_ready, xo_ready, xr_ready, res_ready, act_own = (m.sem(n) for n in ("gy_ready", "xo_ready", "xr_ready", "res_ready", "act_own"))
        blk = m.block()
        rows = t["rows"]
        N_LOAD = 8
        x_src = t["x_in"] if lay == 0 else t["x_mid"]
        done = res_ready if last else xo_ready

        @blk.sync
        def _(sp):
            sp.dma_start(w[:], t["w_out"][lay]).then_inc(par_loaded, 16)
            for dst, n in ((ident, "ident"), (mean_w, "mean_w"), (fnw, "fnw")):
                sp.dma_start(dst[:], t[n]).then_inc(par_loaded, 16)
            for dst, n in ((ln_w, "ln_w"), (ln_b, "ln_b"), (dn_w, "dn_w")):
                sp.dma_start(dst[:], t[n][lay]).then_inc(par_loaded, 16)
            for c in range(2):
                for a in range(2):
                    sp.dma_start(gate[:, c, 512 * a:512 * a + 512], t["mod"][6 * lay + 4 + a, c].partition_broadcast(P)).then_inc(par_loaded, 16)

            def load(b, tok, col):
                for dst, src in ((u, rows[A_CONV[0]:A_CONV[1] + 1:6]), (za, rows[Z_SLICE[0]:Z_SLICE[1] + 1]), (zb, None)):
                    if src is None:
                        sp.dma_start(zb[b][:, 0:2, :], rows[4:6, :, bass.ds(col, P)].rearrange("s p n -> p s n")).then_inc(loaded[b], 16)
                        sp.dma_start(zb[b][:, 2:3, :], rows[8:9, :, bass.ds(col, P)].rearrange("s p n -> p s n")).then_inc(loaded[b], 16)
                    else:
                        sp.dma_start(dst[b][:], src[:, :, bass.ds(col, P)].rearrange("s p n -> p s n")).then_inc(loaded[b], 16)
                sp.dma_start(y[b][:, 5:8, :], t["yc"][:, :, bass.ds(tok, P)].rearrange("s p n -> p s n")).then_inc(loaded[b], 16)
                for d, dst in enumerate((of, ob)):
                    sp.dma_start(dst[b][:].rearrange("p h c -> p (h c)"), t["scan"][d, bass.ds(tok, P), :]).then_inc(loaded[b], 16)
                sp.dma_start(x[b][:], x_src[bass.ds(tok, P), :]).then_inc(loaded[b], 16)

            def store(n, b, tok):
                sp.wait_ge(done, n + 1)
                if last:
                    sp.dma_start(t["out"][bass.ds(tok - CTX, P), :], res[b][:]).then_inc(stored[b], 16)
                else:
                    sp.dma_start(t["x_mid"][bass.ds(tok, P), :], xo[b][:]).then_inc(stored[b], 16)

            def turn(i, b, off):
                n = i * 2 + b
                tok = n * P + first * P
                sp.wait_ge(out_done, n + 1)
                load(b, tok, tok + off)

            sp.sem_inc(out_done, 2)
            for b in range(2):
                sp.sem_inc(stored[b], 16)
                turn(0, b, C0 if not last else L0 - CTX)
            with sp.Fori(1, n_t // 2) as i:
                for b in range(2):
                    store(i * 2 + b - 2, b, (i * 2 + b - 2 + first) * P)
                    turn(i, b, L0 - CTX)
            for b in range(2):
                store(n_t - 2 + b, b, (n_t - 2 + b + first) * P)
            for b in range(2):
                sp.wait_ge(stored[b], 16 * (n_t // 2 + 1))

        @blk.tensor
        def _(pe):
            pe.wait_ge(par_loaded, 11 * 16)

            def project(n, b, h):
                if h == 0:
                    pe.wait_ge(ya_ready, n + 1)
                    pe.wait_ge(yb_ready, n + 1)
                    pe.wait_ge(gy_ready, n)
                for k in range(KT):
                    mm = pe.matmul(ops[:, b, h, :], y[b][:, k, :], w[:, k, 512 * h:512 * h + 512], start=(k == 0), stop=(k == KT - 1))
                if h == 1:
                    mm.then_inc(out_done, 1)

            def body(n, b, i, before):
                pe.wait_ge(loaded[b], 16 * N_LOAD * (i + 1))
                if before:
                    pe.wait_ge(rs_ready, n)
                for c in range(2):
                    mm = pe.matmul(mps[:, 0, 0:P], mean_w[:], u[b][:, c, :], start=(c == 0), stop=(c == 1))
                mm.then_inc(mean_done, 1)
                if before:
                    project(n - 1, 1 - b, 0)
                pe.wait_ge(usq_ready, n + 1)
                for c in range(2):
                    mm = pe.matmul(mps[:, 1, 0:P], mean_w[:], usq[:, c, :], start=(c == 0), stop=(c == 1))
                mm.then_inc(var_done, 1)
                pe.wait_ge(on_ready, n + 1)
                pe.wait_ge(yb_ready, n)
                for pair in range(NP3):
                    mm = pe.transpose(tps[:, pair * P:(pair + 1) * P], of[b][:, 2 * pair:2 * pair + 2, :].rearrange("p h c -> p (h c)"), ident[:])
                mm.then_inc(turned, 1)
                if before:
                    project(n - 1, 1 - b, 1)

            body(0, 0, 0, False)
            body(1, 1, 0, True)
            with pe.Fori(1, n_t // 2) as i:
                for b in range(2):
                    body(i * 2 + b, b, i, True)
            for h in range(2):
                project(n_t - 1, 1, h)

        @blk.scalar
        def _(act):
            act.wait_ge(par_loaded, 11 * 16)
            act.wait_ge(eps_ready, 1)

            def body(n, b):
                s = Steps(act, act_own, n * (4 if last else 2))
                act.wait_ge(oss_ready, n + 1)
                s.link(act.activation(orn[:], oss[:], ACT.Ln, scale=1.0 / HD, bias=eps[:]))
                act.activation(orn[:], orn[:], ACT.Exp, scale=-0.5).then_inc(orn_ready, 1)
                act.wait_ge(var_done, n + 1)
                s.link(act.activation(rs[:], mps[:, 1, 0:P], ACT.Ln, bias=eps[:]))
                act.activation(rs[:], rs[:], ACT.Exp, scale=-0.5).then_inc(rs_ready, 1)
                act.wait_ge(un_ready, n + 1)
                for c in range(2):
                    ins = act.activation(u[b][:, c, :], u[b][:, c, :], ACT.Silu, scale=ln_w[:, c:c + 1], bias=ln_b[:, c:c + 1])
                ins.then_inc(silu_ready, 1)
                return s

            def final(s, n, b):
                act.wait_ge(xo_ready, n + 1)
                s.link(act.activation(sq[:], xo[b][:], ACT.Square, accum_out=xss[:]))
                s.link(act.activation(xss[:], xss[:], ACT.Ln, scale=1.0 / D, bias=eps[:]))
                act.activation(xss[:], xss[:], ACT.Exp, scale=-0.5).then_inc(xr_ready, 1)

            if last:
                s = body(0, 0)
                act.sem_inc(act_own, 2)
                s = body(1, 1)
                final(s, 0, 0)
                with act.Fori(1, n_t // 2) as i:
                    for b in range(2):
                        n = i * 2 + b
                        s = body(n, b)
                        act.wait_ge(res_ready, n - 1)
                        final(s, n - 1, 1 - b)
                act.wait_ge(res_ready, n_t - 1)
                final(Steps(act, act_own, n_t * 4), n_t - 1, 1)
            else:
                with act.Fori(0, n_t // 2) as i:
                    for b in range(2):
                        body(i * 2 + b, b)

        @blk.gpsimd
        def _(pool):
            pool.wait_ge(par_loaded, 11 * 16)

            def body(n, b, before):
                pool.wait_ge(o_ready, n + 1)
                pool.tensor_tensor(osq[:], of[b][:], of[b][:], ALU.mult).then_inc(osq_ready, 1)
                pool.wait_ge(centred, n + 1)
                pool.tensor_tensor(usq[:], u[b][:], u[b][:], ALU.mult).then_inc(usq_ready, 1)
                pool.wait_ge(silu_ready, n + 1)
                pool.tensor_tensor(y[b][:, 0:2, :], u[b][:], za[b][:], ALU.mult).then_inc(ya_ready, 1)

            with pool.Fori(0, n_t // 2) as i:
                for b in range(2):
                    body(i * 2 + b, b, True)

        @blk.vector
        def _(dve):
            dve.memset(eps[:], EPS).then_inc(eps_ready, 1)
            dve.wait_ge(par_loaded, 11 * 16)

            def gated(n, b, c, i):
                dve.wait_ge(out_done, n + 3)
                dve.wait_ge(xo_ready, n)
                dve.wait_ge(stored[b], 16 * (i + 1))
                dve.tensor_tensor(gy[:], ops[:, b].rearrange("p h c -> p (h c)"), gate[:, c, :], ALU.mult).then_inc(gy_ready, 1)
                dve.wait_ge(gy_ready, n + 1)
                dve.tensor_tensor(xo[b][:], gy[:], x[b][:], ALU.add).then_inc(xo_ready, 1)

            def scaled(n, b, i):
                dve.wait_ge(xr_ready, n + 1)
                dve.wait_ge(stored[b], 16 * (i + 1))
                dve.scalar_tensor_tensor(res[b][:], xo[b][:], xss[:], fnw[:], ALU.mult, ALU.mult).then_inc(res_ready, 1)

            def body(n, b, i, before, c):
                dve.wait_ge(loaded[b], 16 * N_LOAD * (i + 1))
                dve.tensor_tensor(of[b][:], of[b][:], ob[b][:], ALU.add).then_inc(o_ready, 1)
                dve.wait_ge(mean_done, n + 1)
                dve.tensor_tensor(u[b][:], u[b][:], mps[:, 0:1, 0:P].to_broadcast([P, 2, P]), ALU.subtract).then_inc(centred, 1)
                dve.wait_ge(osq_ready, n + 1)
                dve.tensor_reduce(oss[:], osq[:], AX.X, ALU.add).then_inc(oss_ready, 1)
                dve.wait_ge(orn_ready, n + 1)
                dve.tensor_tensor(of[b][:], of[b][:], orn[:].unsqueeze(2).to_broadcast([P, NH, HD]), ALU.mult).then_inc(on_ready, 1)
                dve.wait_ge(rs_ready, n + 1)
                dve.tensor_tensor(u[b][:], u[b][:], rs[:].unsqueeze(1).to_broadcast([P, 2, P]), ALU.mult).then_inc(un_ready, 1)
                dve.wait_ge(turned, n + 1)
                dve.scalar_tensor_tensor(y[b][:, 2:5, :], tps[:, 0:3 * P].rearrange("p (s n) -> p s n", s=3), dn_w[:], zb[b][:],
                                         ALU.mult, ALU.mult).then_inc(yb_ready, 1)
                if before:
                    gated(n - 1, 1 - b, c, i - 1 + b)
                    if last:
                        scaled(n - 1, 1 - b, i - 1 + b)

            c0 = 0 if last else 1
            body(0, 0, 0, False, 0)
            body(1, 1, 0, True, c0)
            body(2, 0, 1, True, c0)
            body(3, 1, 1, True, 0)
            with dve.Fori(2, n_t // 2) as i:
                for b in range(2):
                    body(i * 2 + b, b, i, True, 0)
            gated(n_t - 1, 1, 0, n_t // 2 - 1)
            if last:
                scaled(n_t - 1, 1, n_t // 2 - 1)


def build(nc, t, stages=None):
    modulation(nc, t)
    for lay in range(DEPTH):
        with nc.sbuf_tensor(f"hT{lay}", [P, KT, TOK], F32) as hT:
            normalise(nc, t, lay, hT, t["x_in"] if lay == 0 else t["x_mid"])
            project_a(nc, t, lay, hT)
            project_qkv(nc, t, lay, hT)
            project_c(nc, t, lay, hT)
        if stages == 1:
            return
        gates(nc, t, lay)
        rotate(nc, t, lay)
        deltanet(nc, t, lay)
        for ctx in ((False,) if lay == DEPTH - 1 else (True, False)):
            attention(nc, t, lay, ctx)
        finish(nc, t, lay)
        if stages == 2:
            return


def tiled(w):
    *lead, k, n = w.shape
    w = w.reshape(*lead, k // P, P, n // P, P)
    ax = list(range(len(lead)))
    q = len(lead)
    return np.ascontiguousarray(w.transpose(*ax, q + 2, q + 1, q, q + 3))


def lay_out(a):
    f = {k: np.asarray(v) for k, v in a.items()}
    out = {}
    out["x_in"] = np.concatenate([f["ctx"][0], f["x"][0]], axis=0)
    cond = np.stack([f["c"][0], f["c_ctx"]], axis=-1)
    out["cond"] = np.ascontiguousarray(cond.reshape(KT, P, 2).transpose(1, 0, 2))
    aw = f["ada_w"].reshape(DEPTH, KT, P, 6, 512)
    out["ada_w"] = np.ascontiguousarray(aw.transpose(0, 3, 2, 1, 4).reshape(DEPTH * 6, P, KT, 512))
    out["ada_b"] = np.ascontiguousarray(np.broadcast_to(f["ada_b"][None], (2, DEPTH, 3 * D)))
    out["norm_w"] = np.ascontiguousarray(f["norm_w"].reshape(DEPTH, KT, P).transpose(0, 2, 1))
    q_pairs = [np.r_[j * HD:(j + 1) * HD, (j + 3) * HD:(j + 4) * HD] for j in range(3)]
    z = [512 + np.arange(P), 640 + np.arange(P)] + [1920 + P * i + np.arange(P) for i in range(3)] + [2968 + q for q in q_pairs]
    cols = []
    for c in range(2):
        cols += [P * c + np.arange(P), 256 + P * c + np.arange(P)] + z[4 * c:4 * c + 4]
    for i in range(3):
        cols += [768 + P * i + np.arange(P), 1152 + P * i + np.arange(P), 1536 + P * i + np.arange(P)]
    cols += [2328 + q for q in q_pairs] + [2712 + np.arange(P), 2840 + np.arange(P), 2304 + np.arange(24)]
    w = f["w_in"][:, :, np.concatenate(cols)]
    w = np.concatenate([w, np.zeros((DEPTH, D, (NS + 2) * P - w.shape[2]), np.float32)], axis=2)
    out["w_in"] = tiled(w)
    ca = np.concatenate([f["conv_a_w"], f["conv_a_b"][:, None]], axis=1)
    out["conv_a"] = np.ascontiguousarray(ca.reshape(DEPTH, CW_A + 1, 2, P).transpose(0, 3, 2, 1))
    cb = f["qkv_conv_w"].reshape(DEPTH, CW_B, 3, 3, P)
    out["conv_b"] = np.ascontiguousarray(cb.transpose(0, 4, 3, 2, 1).reshape(DEPTH, P, 9, CW_B))
    every = lambda x: np.ascontiguousarray(np.broadcast_to(x[:, None], (x.shape[0], P, *x.shape[1:])))
    out["dt_bias"], out["a_log"], out["sink"] = every(f["dt_bias"]), every(f["a_log"]), every(f["sink"])
    out["fnw"] = np.ascontiguousarray(np.broadcast_to(f["final_norm_w"], (P, D)))
    out["ln_w"], out["ln_b"] = (np.ascontiguousarray(f[n].reshape(DEPTH, 2, P).transpose(0, 2, 1)) for n in ("ln_a_w", "ln_a_b"))
    out["dn_w"] = np.ascontiguousarray(np.tile(f["dn_norm_w"], (1, 2))[:, :, None])
    order = np.r_[0:640, np.concatenate([640 + q for q in q_pairs])]
    out["w_out"] = np.ascontiguousarray(f["w_out"][:, order].reshape(DEPTH, KT, P, D).transpose(0, 2, 1, 3))
    out.update(constants())
    return out


def constants():
    c = {}
    c["ident"] = np.eye(P, dtype=np.float32)
    c["blockdiag"] = np.kron(np.eye(2, dtype=np.float32), np.ones((HD, HD), np.float32))
    c["ones"] = np.ones((P, HD), np.float32)
    c["mean_w"] = np.full((P, P), 1.0 / (2 * P), np.float32)
    f = np.arange(P) % HD
    freq = (10000.0 ** (-np.arange(16, dtype=np.float32) / 16)).astype(np.float32)[f % 16]
    pos = np.arange(SEQ)
    where = np.where((f // 32 == 0)[:, None], pos // 64, pos % 64).astype(np.float32)
    ang = where * freq[:, None]
    c["cos"] = np.cos(ang).astype(np.float32)
    c["sin"] = (np.sin(ang) * np.where(f % 32 < 16, -1, 1)[:, None]).astype(np.float32)
    c["swap"] = np.eye(P, dtype=np.float32)[np.arange(P) ^ 16]
    qi, ki = np.arange(P)[:, None], np.arange(P)[None]
    left, right = np.where(ki >= qi, 0, NEG), np.where(ki <= qi, 0, NEG)
    mask = np.stack([np.concatenate([left, right], 1)] * (SEQ // P)).astype(np.float32)
    mask[0, :, :P] = NEG
    mask[-1, :, P:] = NEG
    c["mask"] = mask
    a, b = np.arange(CH)[:, None], np.arange(CH)[None]
    both = lambda fwd: np.concatenate([fwd(a, b), fwd(-a, -b)]).astype(np.float32)
    c["tri_c"] = both(lambda i, j: i <= j)
    c["tri"] = (np.concatenate([c["tri_c"]] * 2, axis=1) * c["blockdiag"]).astype(np.float32)
    c["negmask"] = np.where(c["tri_c"] > 0, 0, NEG).astype(np.float32)
    c["eye_c"] = np.concatenate([np.eye(CH, dtype=np.float32)] * 2)
    c["dirmask"] = np.kron(np.eye(2, dtype=np.float32), np.ones((CH, 1), np.float32))
    below = lambda s: np.concatenate([(a // s % 2 == 1) & (b // s == a // s - 1),
                                      (b // s % 2 == 1) & (a // s == b // s - 1)]).astype(np.float32)
    c["lmask"] = np.ascontiguousarray(np.stack([below(s) for s in (1, 2, 4, 8, 16, 32)], axis=1))
    m1 = below(1).reshape(2, CH, CH)
    c["umask1"] = np.ascontiguousarray(m1.transpose(0, 2, 1).reshape(P, CH))
    return c


SCRATCH = {
    "gates": (TOK, 4 * NH),
    "qk": (4, P, TOK + KPAD),
    "vt": (NT + 1, P, P),
    "yc": (3, P, TOK),
    "scan": (2, TOK, NH * HD),
    "mod": (DEPTH * 6, 2, 512),
    "rows": (NS, P, RL),
    "x_mid": (TOK, D),
}


def program(nc, shapes, debug=(), stages=None):
    t = {n: nc.dram_tensor(f"in_{n}", shape, F32, kind="ExternalInput").ap() for n, shape in shapes.items()}
    for n, shape in SCRATCH.items():
        t[n] = nc.dram_tensor(n, shape, F32, kind="ExternalOutput" if n in debug else "Internal").ap()
    t["out"] = nc.dram_tensor("out_0", (SEQ, D), F32, kind="ExternalOutput").ap()
    build(nc, t, stages)


def kernel(**inputs):
    import concourse.bacc as _bacc
    from concourse.bass_utils import run_bass_kernel_spmd as _run

    arrays = lay_out(inputs)
    nc = _bacc.Bacc("TRN2", target_bir_lowering=False, num_devices=1)
    program(nc, {n: a.shape for n, a in arrays.items()})
    r = _run(nc, [{f"in_{n}": a for n, a in arrays.items()}], core_ids=[0])
    return r.results[0]["out_0"].reshape(1, SEQ, D)
```

```python
from contextlib import ExitStack

import numpy as np

import concourse.bass as bass
from concourse import mybir

F32 = mybir.dt.float32
F32R = mybir.dt.float32r
ALU = mybir.AluOpType
ACT = mybir.ActivationFunctionType
AX = mybir.AxisListType

P = 128
D = 1024
KT = D // P
DEPTH = 2
CTX, SEQ = 256, 2048
TOK = CTX + SEQ
NT = TOK // P
NCT = CTX // P
HD = 64
NH = 6
NP3 = NH // 2
CW_A, CW_B = 31, 5
PADC = (CW_A - 1) // 2
RL = 2352
C0 = PADC
L0 = PADC + CTX + PADC
CONV_N = CTX + PADC + SEQ
KPAD = P
EPS = 1e-6
CH = 64
NSTEP = TOK // CH
NCSTEP = CTX // CH
NEG = -1.0e30

S_A = 0
S_QKV = 12
S_QC = 21
S_KC, S_VC, S_SC = 24, 25, 26
NS = 27
Z_SLICE = [2, 3, 4, 5, 8, 9, 10, 11]
A_CONV = [0, 6]

GROUPS = [(0, CTX, C0)] + [(CTX + 512 * g, 512, L0 + 512 * g) for g in range(SEQ // 512)]
NG = len(GROUPS)


class Steps:

    def __init__(self, eng, sem, at=0):
        self.eng, self.sem, self.at, self.n = eng, sem, at, 0

    def inc(self, ins):
        self.n += 1
        return ins.then_inc(self.sem, 1)

    def link(self, ins):
        self.inc(ins)
        self.eng.wait_ge(self.sem, self.at + self.n)


class Mem:

    def __init__(self, nc, tag):
        self.nc, self.tag, self.stack, self.taken = nc, tag, ExitStack(), []

    def __enter__(self):
        self.stack.__enter__()
        return self

    def __exit__(self, *a):
        self.stack.__exit__(*a)
        self.nc.clear_and_free_semaphores(self.taken)
        self.nc.all_engine_barrier()

    def sb(self, name, *shape):
        return self.stack.enter_context(self.nc.sbuf_tensor(f"{self.tag}_{name}", [P, *shape], F32))

    def sb_r(self, name, *shape):
        return self.stack.enter_context(self.nc.sbuf_tensor(f"{self.tag}_{name}", [P, *shape], F32R))

    def ps(self, name, *shape):
        return self.stack.enter_context(self.nc.psum_tensor(f"{self.tag}_{name}", [P, *shape], F32))

    def sem(self, name):
        self.taken.append(self.nc.alloc_semaphore(f"{self.tag}_{name}"))
        return self.taken[-1]

    def sems(self, name, n):
        return [self.sem(f"{name}{i}") for i in range(n)]

    def block(self):
        return self.stack.enter_context(self.nc.Block())


def split_in_two(eng, x, hi, lo, split, n):
    eng.tensor_copy(hi, x).then_inc(split, 1)
    eng.wait_ge(split, n + 1)
    return eng.tensor_tensor(lo, x, hi.bitcast(F32), ALU.subtract)


def in_parts(pe, out, lhs, rhs, ks=range(KT)):
    for k in ks:
        (lh, ll), (rh, rl) = lhs(k), rhs(k)
        pe.matmul(out, lh, rh, start=(k == 0), stop=False)
        pe.matmul(out, lh, rl, start=False, stop=False)
        mm = pe.matmul(out, ll, rh, start=False, stop=(k == KT - 1))
    return mm


def ds1(i):
    return bass.ds(i, 1)


def modulation(nc, t):
    NB = 3 * D // 512
    NW = 4
    with Mem(nc, "ada") as m:
        cond = m.sb("cond", KT, 2)
        scond = m.sb("scond", KT, 2)
        w = [m.sb(f"w{b}", KT, 512) for b in range(NW)]
        bias = m.sb("bias", DEPTH, 3 * D)
        out = [m.sb(f"out{b}", 512) for b in range(NW)]
        acc = m.ps("acc", NW, 512)
        in_loaded, cond_ready = m.sem("in_loaded"), m.sem("cond_ready")
        w_loaded, out_stored = m.sems("w_loaded", NW), m.sems("out_stored", NW)
        acc_ready, out_ready = m.sem("acc_ready"), m.sem("out_ready")
        blk = m.block()
        n_it = DEPTH * NB
        w_src = t["ada_w"]

        @blk.sync
        def _(sp):
            sp.dma_start(cond[:], t["cond"]).then_inc(in_loaded, 16)
            sp.dma_start(bias[0:2], t["ada_b"]).then_inc(in_loaded, 16)
            for b in range(NW):
                sp.dma_start(w[b][:], w_src[b]).then_inc(w_loaded[b], 16)
            for b in range(NW):
                sp.sem_inc(out_stored[b], 16)
            def store(it, b):
                sp.wait_ge(out_ready, it + 1)
                sp.dma_start(t["mod"][ds1(it)].rearrange("a c n -> c (a n)"), out[b][0:2]).then_inc(out_stored[b], 16)

            with sp.Fori(0, n_it // NW - 1) as i:
                for b in range(NW):
                    store(i * NW + b, b)
                    sp.dma_start(w[b][:], w_src[ds1(i * NW + (b + NW))].rearrange("a p k n -> p (a k) n")).then_inc(w_loaded[b], 16)
            for b in range(NW):
                store(n_it - NW + b, b)
            for b in range(NW):
                sp.wait_ge(out_stored[b], 16 * (n_it // NW + 1))

        @blk.scalar
        def _(act):
            act.wait_ge(in_loaded, 32)
            act.activation(scond[:], cond[:], ACT.Silu).then_inc(cond_ready, 1)

        @blk.tensor
        def _(pe):
            pe.wait_ge(cond_ready, 1)
            with pe.Fori(0, n_it // NW) as i:
                for b in range(NW):
                    pe.wait_ge(w_loaded[b], 16 * (i + 1))
                    for k in range(KT):
                        mm = pe.matmul(acc[0:2, b, :], scond[:, k, :], w[b][:, k, :], start=(k == 0), stop=(k == KT - 1))
                    mm.then_inc(acc_ready, 1)

        @blk.vector
        def _(dve):
            dve.wait_ge(in_loaded, 32)
            for it in range(n_it):
                b = it % NW
                dve.wait_ge(acc_ready, it + 1)
                dve.wait_ge(out_stored[b], 16 * (it // NW + 1))
                dve.tensor_tensor(out[b][0:2], acc[0:2, b, :], bias[0:2, it // NB, 512 * (it % NB):512 * (it % NB) + 512],
                                  ALU.add).then_inc(out_ready, 1)


def normalise(nc, t, lay, h_hi, h_lo, x_src):
    NB = 4
    with Mem(nc, f"nrm{lay}") as m:
        ident = m.sb("ident", P)
        nw = m.sb("nw", KT)
        scale, shift, wsc = m.sb("scale", 2, KT), m.sb("shift", 2, KT), m.sb("wsc", 2, KT)
        eps = m.sb("eps", 1)
        x = [m.sb(f"x{b}", D) for b in range(NB)]
        xn = [m.sb(f"xn{b}", D) for b in range(NB)]
        h = [m.sb(f"h{b}", KT, P) for b in range(2)]
        sq = m.sb("sq", D)
        ss, rms, rstd = (m.sb(n, NB) for n in ("ss", "rms", "rstd"))
        tp = m.ps("tp", 2, KT, P)
        par_loaded, mod_loaded, eps_ready, wsc_ready = (m.sem(n) for n in ("par_loaded", "mod_loaded", "eps_ready", "wsc_ready"))
        x_loaded = m.sems("x_loaded", NB)
        ss_ready, rms_ready, rstd_ready, xn_ready = (m.sem(n) for n in ("ss_ready", "rms_ready", "rstd_ready", "xn_ready"))
        turned, dve_out, act_out = m.sem("turned"), m.sem("dve_out"), m.sem("act_out")
        hi_ready, lo_ready = m.sem("hi_ready"), m.sem("lo_ready")
        blk = m.block()
        n_act = KT // 2

        def each_tile(eng, turn):
            for n in range(NCT):
                turn(n, n, 0, 1)
            with eng.Fori(0, (NT - NCT) // NB) as i:
                for j in range(NB):
                    turn(i * NB + (NCT + j), (NCT + j) % NB, i + (NCT + j) // NB, 0)

        @blk.sync
        def _(sp):
            for n in range(NB):
                sp.dma_start(x[n][:], x_src[n * P:(n + 1) * P, :]).then_inc(x_loaded[n], 16)
            sp.dma_start(ident[:], t["ident"]).then_inc(par_loaded, 16)
            sp.dma_start(nw[:], t["norm_w"][lay]).then_inc(mod_loaded, 16)
            for c in range(2):
                for k in range(2):
                    src = t["mod"][6 * lay + 2 * k:6 * lay + 2 * k + 2, c:c + 1, :]
                    for a in range(2):
                        sp.dma_start((shift, scale)[k][:, c, 4 * a:4 * a + 4], src[a, 0].rearrange("(k p) -> p k", p=P),
                                     allow_slow_non_contiguous=True).then_inc(mod_loaded, 16)

            def reload(n, b):
                sp.wait_ge(xn_ready, n + 1)
                sp.dma_start(x[b][:], x_src[bass.ds((n + NB) * P, P), :]).then_inc(x_loaded[b], 16)

            n_loop = (NT - NB) // NB
            with sp.Fori(0, n_loop) as i:
                for b in range(NB):
                    reload(i * NB + b, b)
            for n in range(n_loop * NB, NT - NB):
                reload(n, n % NB)

        @blk.vector
        def _(dve):
            dve.memset(eps[:], EPS).then_inc(eps_ready, 1)
            dve.wait_ge(mod_loaded, 9 * 16)
            for c in range(2):
                dve.scalar_tensor_tensor(wsc[:, c, :], scale[:, c, :], 1.0, nw[:], ALU.add, ALU.mult).then_inc(wsc_ready, 1)
            dve.wait_ge(wsc_ready, 2)

            def inverse(n, b):
                dve.wait_ge(rms_ready, n + 1)
                dve.reciprocal(rstd[:, b:b + 1], rms[:, b:b + 1]).then_inc(rstd_ready, 1)

            def turn(n, b, turns, c, ahead=True):
                if ahead:
                    inverse(n + 1, (b + 1) % NB)
                dve.wait_ge(turned, n + 1)
                for k in range(n_act, KT):
                    ins = dve.tensor_scalar(h[b % 2][:, k, :], tp[:, b % 2, k, :],
                                            wsc[:, c, k:k + 1], shift[:, c, k:k + 1], ALU.mult, ALU.add)
                ins.then_inc(dve_out, 1)
                dve.wait_ge(hi_ready, n + 1)
                cols = bass.ds(n * P, P)
                dve.tensor_tensor(h_lo[:, :, cols], h[b % 2][:], h_hi[:, :, cols].bitcast(F32), ALU.subtract).then_inc(lo_ready, 1)

            inverse(0, 0)
            for n in range(NCT):
                turn(n, n, 0, 1)
            with dve.Fori(0, (NT - NCT) // NB - 1) as i:
                for j in range(NB):
                    turn(i * NB + (NCT + j), (NCT + j) % NB, None, 0)
            for n in range(NT - NB, NT):
                turn(n, n % NB, None, 0, n + 1 < NT)

        @blk.scalar
        def _(act):
            act.wait_ge(eps_ready, 1)

            def root(n, b, turns):
                act.wait_ge(x_loaded[b], 16 * (turns + 1))
                act.activation(sq[:], x[b][:], ACT.Square, accum_out=ss[:, b:b + 1]).then_inc(ss_ready, 1)
                act.wait_ge(ss_ready, n + 1)
                act.activation(rms[:, b:b + 1], ss[:, b:b + 1], ACT.Sqrt, scale=1.0 / D, bias=eps[:]).then_inc(rms_ready, 1)

            def out(n, b, c):
                act.wait_ge(turned, n + 1)
                if not (isinstance(n, int) and n < 2):
                    act.wait_ge(lo_ready, n - 1)
                for k in range(n_act):
                    ins = act.activation(h[b % 2][:, k, :], tp[:, b % 2, k, :], ACT.Identity,
                                         scale=wsc[:, c, k:k + 1], bias=shift[:, c, k:k + 1])
                ins.then_inc(act_out, 1)
                act.wait_ge(act_out, n + 3)
                act.wait_ge(dve_out, n + 3)
                act.activation(h_hi[:, :, bass.ds(n * P, P)], h[b % 2][:], ACT.Copy).then_inc(hi_ready, 1)

            def turn(n, b, turns, c, ahead=True):
                if ahead:
                    root(n + 1, (b + 1) % NB, turns + (b + 1) // NB)
                out(n, b, c)

            root(0, 0, 0)
            act.wait_ge(wsc_ready, 2)
            for n in range(NCT):
                turn(n, n, 0, 1)
            with act.Fori(0, (NT - NCT) // NB - 1) as i:
                for j in range(NB):
                    turn(i * NB + (NCT + j), (NCT + j) % NB, i + (NCT + j) // NB, 0)
            for n in range(NT - NB, NT):
                turn(n, n % NB, n // NB, 0, n + 1 < NT)

        @blk.gpsimd
        def _(pool):
            def turn(n, b, turns, c):
                pool.wait_ge(rstd_ready, n + 1)
                if not (isinstance(n, int) and n < NB):
                    pool.wait_ge(turned, n - (NB - 1))
                pool.tensor_tensor(xn[b][:], x[b][:], rstd[:, b:b + 1].to_broadcast([P, D]), ALU.mult).then_inc(xn_ready, 1)

            for n in range(NB):
                turn(n, n, 0, None)
            with pool.Fori(1, NT // NB) as i:
                for j in range(NB):
                    turn(i * NB + j, j, None, None)
            for n in range(NT // NB * NB, NT):
                turn(n, n % NB, None, None)

        @blk.tensor
        def _(pe):
            pe.sem_inc(dve_out, 2)
            pe.sem_inc(act_out, 2)
            pe.wait_ge(par_loaded, 16)

            def turn(n, b, turns, c):
                pe.wait_ge(xn_ready, n + 1)
                pe.wait_ge(dve_out, n + 1)
                pe.wait_ge(act_out, n + 1)
                for k in range(KT):
                    mm = pe.transpose(tp[:, b % 2, k, :], xn[b][:, k * P:(k + 1) * P], ident[:])
                mm.then_inc(turned, 1)

            each_tile(pe, turn)


def project_slice(pe, s, w, h, acc, acc_free, acc_ready):
    for g, (t0, n, _) in enumerate(GROUPS):
        pe.wait_ge(acc_free, s * NG + g + 1)
        in_parts(pe, acc[:, g, 0:n], lambda k: (w[0][:, k, :], w[1][:, k, :]),
                 lambda k: (h[0][:, k, t0:t0 + n], h[1][:, k, t0:t0 + n])).then_inc(acc_ready, 1)


def take_out(act, s, acc, acc_ready, acc_free, row, func):
    for g, (_, n, col) in enumerate(GROUPS):
        act.wait_ge(acc_ready, s * NG + g + 1)
        ins = act.activation(row[:, col:col + n], acc[:, g, 0:n], func)
        ins.then_inc(acc_free, 1)
    return ins


def zero_pads(eng, rows, sem):
    for r in rows:
        for lo, hi in ((0, C0), (C0 + CTX, L0), (L0 + SEQ, RL)):
            eng.memset(r[:, lo:hi], 0.0).then_inc(sem, 1)


class Weights:

    def __init__(self, m):
        self.raw = m.sb("w_raw", KT, P)
        self.parts = [(m.sb_r(f"w_hi{b}", KT, P), m.sb_r(f"w_lo{b}", KT, P)) for b in range(2)]
        self.loaded, self.rounded, self.ready, self.waits_passed = (m.sem(n) for n in ("w_loaded", "w_rounded", "w_ready", "w_waits_passed"))

    def split(self, pool, s, b):
        pool.wait_ge(self.loaded, 16 * (s + 1))
        pool.sem_inc(self.waits_passed, 1)
        hi, lo = self.parts[b]
        split_in_two(pool, self.raw[:], hi[:], lo[:], self.rounded, s).then_inc(self.ready, 1)

    def load(self, sp, src, s):
        if not isinstance(s, int) or s > 0:
            sp.wait_ge(self.ready, s)
        sp.dma_start(self.raw[:], src).then_inc(self.loaded, 16)


def project_a(nc, t, lay, h, w):
    with Mem(nc, f"pa{lay}") as m:
        u, gate, conv, z = (m.sb(n, RL) for n in ("u", "gate", "conv", "z"))
        taps = m.sb("taps", 2, CW_A + 1)
        acc = m.ps("acc", NG, 512)
        z_stored, taps_loaded, pads = m.sem("z_stored"), m.sem("taps_loaded"), m.sem("pads")
        acc_ready, acc_free, row_ready = m.sem("acc_ready"), m.sem("acc_free"), m.sem("row_ready")
        u_ready, conv_own, conv_ready, conv_stored = (m.sem(n) for n in ("u_ready", "conv_own", "conv_ready", "conv_stored"))
        blk = m.block()
        rows = t["rows"]
        NI = 6

        @blk.sync
        def _(sp):
            w.load(sp, t["w_in"][lay, 0], 0)
            sp.dma_start(taps[:], t["conv_a"][lay]).then_inc(taps_loaded, 16)
            w.load(sp, t["w_in"][lay, 1], 1)
            with sp.Fori(0, 2) as i:
                for j in range(NI):
                    s = i * NI + j
                    w.load(sp, t["w_in"][lay, ds1(s + 2)].rearrange("a p k n -> p (a k) n"), s + 2)
                    if j >= 2:
                        sp.wait_ge(row_ready, s + 1)
                        sp.dma_start(rows[ds1(s)].rearrange("a p n -> p (a n)"), z[:]).then_inc(z_stored, 16)
                sp.wait_ge(conv_ready, i + 2)
                sp.dma_start(rows[ds1(i * NI)].rearrange("a p n -> p (a n)"), conv[:]).then_inc(conv_stored, 16)
            sp.wait_ge(conv_stored, 3 * 16)
            sp.wait_ge(z_stored, 9 * 16)
            sp.wait_ge(w.loaded, (2 * NI + 2) * 16)

        @blk.tensor
        def _(pe):
            pe.sem_inc(acc_free, NG)
            with pe.Fori(0, 2) as i:
                for j in range(NI):
                    pe.wait_ge(w.ready, i * NI + j + 1)
                    project_slice(pe, i * NI + j, w.parts[j % 2], h, acc, acc_free, acc_ready)

        @blk.scalar
        def _(act):
            act.sem_inc(z_stored, 16)
            act.sem_inc(u_ready, 1)
            act.wait_ge(pads, 4 * 3)
            with act.Fori(0, 2) as i:
                for j in range(NI):
                    if j == 0:
                        act.wait_ge(conv_ready, i + 1)
                    if j == 1:
                        act.wait_ge(u_ready, i + 1)
                    if j >= 2:
                        act.wait_ge(z_stored, 16 * (i * 4 + j - 1))
                    row, func = ((u, ACT.Copy), (gate, ACT.Sigmoid))[j] if j < 2 else (z, ACT.Silu)
                    take_out(act, i * NI + j, acc, acc_ready, acc_free, row, func)
                    act.wait_ge(acc_free, (i * NI + j + 2) * NG)
                    act.sem_inc(row_ready, 1)

        @blk.gpsimd
        def _(pool):
            w.split(pool, 0, 0)
            zero_pads(pool, (u, gate, conv, z), pads)
            with pool.Fori(0, 2) as i:
                for j in range(NI):
                    pool.wait_ge(acc_free, (i * NI + j + 1) * NG)
                    w.split(pool, i * NI + j + 1, (j + 1) % 2)
                    if j == 2:
                        pool.wait_ge(row_ready, i * NI + 2)
                        pool.tensor_tensor(u[:, C0:C0 + CONV_N], u[:, C0:C0 + CONV_N], gate[:, C0:C0 + CONV_N], ALU.mult).then_inc(u_ready, 1)

        @blk.vector
        def _(dve):
            dve.sem_inc(conv_stored, 16)
            dve.sem_inc(conv_ready, 1)
            dve.wait_ge(taps_loaded, 16)
            dve.wait_ge(pads, 4 * 3)
            for i in range(2):
                dve.wait_ge(u_ready, i + 2)
                dve.wait_ge(conv_stored, 16 * (i + 1))
                s = Steps(dve, conv_own, i * CW_A)
                out = conv[:, C0:C0 + CONV_N]
                s.link(dve.tensor_scalar(out, u[:, 0:CONV_N], taps[:, i, 0:1], taps[:, i, CW_A:CW_A + 1], ALU.mult, ALU.add))
                for k in range(1, CW_A):
                    s.link(dve.scalar_tensor_tensor(out, u[:, k:k + CONV_N], taps[:, i, k:k + 1], out, ALU.mult, ALU.add))
                dve.sem_inc(conv_ready, 1)


NB_N = 3


def project_qkv(nc, t, lay, h, w):
    with Mem(nc, f"pq{lay}") as m:
        ROW = (0, 1, 0)
        raw = [m.sb(f"raw{b}", RL) for b in range(2)]
        con = [m.sb(f"con{b}", RL) for b in range(2)]
        taps = m.sb("taps", 9, CW_B)
        heads = m.sb("heads", P)
        eps = m.sb("eps", 2)
        acc = m.ps("acc", NG, 512)
        nps = m.ps("nps", NB_N, 512)
        stored = m.sems("stored", 2)
        par_loaded, pads = m.sem("par_loaded"), m.sem("pads")
        acc_ready, acc_free, row_ready = m.sem("acc_ready"), m.sem("acc_free"), m.sem("row_ready")
        dve_own, conv_ready, silu_ready, sq_ready = (m.sem(n) for n in ("dve_own", "conv_ready", "silu_ready", "sq_ready"))
        norm_ready, ln_ready, rn_ready, unit_ready = (m.sem(n) for n in ("norm_ready", "ln_ready", "rn_ready", "unit_ready"))
        blk = m.block()
        rows = t["rows"]
        wide = slice(C0, C0 + CONV_N)
        STREAMS = (slice(C0, C0 + CTX), slice(L0, L0 + SEQ))
        DVE_OWN = 3 * CW_B + 2
        OFF = (CW_A - CW_B) // 2

        @blk.sync
        def _(sp):
            sp.dma_start(taps[:], t["conv_b"][lay]).then_inc(par_loaded, 16)
            sp.dma_start(heads[:], t["blockdiag"]).then_inc(par_loaded, 16)
            w.load(sp, t["w_in"][lay, S_QKV + 2], S_QKV + 2)
            with sp.Fori(0, 3) as i:
                def load(j):
                    w.load(sp, t["w_in"][lay, ds1(i * 3 + (S_QKV + 3 + j))].rearrange("a p k n -> p (a k) n"), i * 3 + (S_QKV + 3 + j))

                def store(j):
                    sp.wait_ge(*((silu_ready, 3 * i + 3) if j == 2 else (unit_ready, 2 * i + j + 1)))
                    sp.dma_start(rows[ds1(i * 3 + (S_QKV + j))].rearrange("a p n -> p (a n)"), con[ROW[j]][:]).then_inc(stored[ROW[j]], 16)

                load(0)
                store(0)
                load(1)
                load(2)
                store(1)
                store(2)
            sp.wait_ge(stored[0], 7 * 16)
            sp.wait_ge(stored[1], 4 * 16)
            sp.wait_ge(w.loaded, (S_QC + 3) * 16)

        @blk.tensor
        def _(pe):
            pe.sem_inc(acc_free, NG)
            pe.wait_ge(par_loaded, 32)

            def norms(n, j):
                pe.wait_ge(sq_ready, n + 1)
                for g, (_, cnt, col) in enumerate(GROUPS):
                    q = n * NG + g
                    pe.wait_ge(ln_ready, q + 1)
                    pe.matmul(nps[:, g % NB_N, 0:cnt], heads[:], raw[j][:, col:col + cnt],
                              start=True, stop=True).then_inc(norm_ready, 1)

            pe.sem_inc(ln_ready, 2)
            with pe.Fori(0, 3) as i:
                for j in range(3):
                    pe.wait_ge(w.ready, i * 3 + (S_QKV + j + 1))
                    project_slice(pe, i * 3 + j, w.parts[ROW[j]], h, acc, acc_free, acc_ready)
                    if j >= 1:
                        norms(i * 2 + j - 1, j - 1)

        @blk.scalar
        def _(act):
            act.sem_inc(dve_own, 1)
            for b in range(2):
                act.sem_inc(stored[b], 16)
            act.wait_ge(pads, 4 * 3 + 2)

            def take(i, j):
                if j == 2:
                    act.wait_ge(unit_ready, 2 * i + 1)
                else:
                    act.wait_ge(dve_own, i * DVE_OWN + 1)
                take_out(act, i * 3 + j, acc, acc_ready, acc_free, raw[ROW[j]], ACT.Copy)
                act.wait_ge(acc_free, (i * 3 + j + 2) * NG)
                act.sem_inc(row_ready, 1)

            def silu(i, j):
                act.wait_ge(conv_ready, i * 3 + j + 1)
                for part in STREAMS:
                    ins = act.activation(con[ROW[j]][:, part], con[ROW[j]][:, part], ACT.Silu)
                ins.then_inc(silu_ready, 1)

            def inverse_norm(i, j):
                for g, (_, n, col) in enumerate(GROUPS):
                    q = (i * 2 + j) * NG + g
                    act.wait_ge(norm_ready, q + 1)
                    act.activation(raw[j][:, col:col + n], nps[:, g % NB_N, 0:n], ACT.Ln,
                                   scale=(float(HD), 1.0)[j], bias=eps[:, j:j + 1]).then_inc(ln_ready, 1)
                act.wait_ge(ln_ready, (i * 2 + j + 1) * NG + 2)
                for part in STREAMS:
                    ins = act.activation(raw[j][:, part], raw[j][:, part], ACT.Exp, scale=-0.5)
                ins.then_inc(rn_ready, 1)

            with act.Fori(0, 3) as i:
                take(i, 0)
                silu(i, 0)
                take(i, 1)
                inverse_norm(i, 0)
                silu(i, 1)
                take(i, 2)
                inverse_norm(i, 1)
                silu(i, 2)

        @blk.gpsimd
        def _(pool):
            zero_pads(pool, (*raw, *con), pads)
            pool.memset(eps[:, 0:1], EPS * HD).then_inc(pads, 1)
            pool.memset(eps[:, 1:2], EPS).then_inc(pads, 1)
            w.split(pool, S_QKV + 1, 1)
            with pool.Fori(0, 3) as i:
                pool.wait_ge(acc_ready, (i * 3 + 1) * NG)
                w.split(pool, i * 3 + (S_QKV + 2), 0)
                for j in range(2):
                    pool.wait_ge(silu_ready, i * 3 + j + 1)
                    for part in STREAMS:
                        ins = pool.tensor_tensor(raw[j][:, part], con[j][:, part], con[j][:, part], ALU.mult)
                    ins.then_inc(sq_ready, 1)
                pool.wait_ge(acc_ready, (i * 3 + 3) * NG)
                for j in range(2):
                    w.split(pool, i * 3 + (S_QKV + 3 + j), j)

        @blk.vector
        def _(dve):
            dve.wait_ge(par_loaded, 32)
            dve.wait_ge(pads, 4 * 3 + 2)
            for i in range(3):
                s = Steps(dve, dve_own, i * DVE_OWN + 1)

                def conv(j):
                    b = ROW[j]
                    dve.wait_ge(row_ready, i * 3 + j + 1)
                    dve.wait_ge(stored[b], 16 * (i + 1 if j == 1 else 2 * i + 1 + j // 2))
                    out = con[b][:, wide]
                    s.link(dve.tensor_scalar(out, raw[b][:, OFF:OFF + CONV_N], taps[:, 3 * i + j, 0:1], None, ALU.mult))
                    for k in range(1, CW_B):
                        s.link(dve.scalar_tensor_tensor(out, raw[b][:, OFF + k:OFF + k + CONV_N], taps[:, 3 * i + j, k:k + 1],
                                                        out, ALU.mult, ALU.add))
                    dve.sem_inc(conv_ready, 1)

                def unit(j):
                    dve.wait_ge(rn_ready, 2 * i + j + 1)
                    s.link(dve.tensor_tensor(con[j][:, wide], con[j][:, wide], raw[j][:, wide], ALU.mult))
                    dve.sem_inc(unit_ready, 1)

                conv(0)
                conv(1)
                unit(0)
                conv(2)
                unit(1)


def project_c(nc, t, lay, h, w):
    with Mem(nc, f"pc{lay}") as m:
        row = [m.sb(f"row{b}", RL) for b in range(2)]
        acc = m.ps("acc", NG, 512)
        stored, pads = m.sems("stored", 2), m.sem("pads")
        acc_ready, acc_free, row_ready = m.sem("acc_ready"), m.sem("acc_free"), m.sem("row_ready")
        blk = m.block()
        n_s = NS - S_QC

        @blk.sync
        def _(sp):
            for s in range(n_s):
                if s + 3 < n_s:
                    w.load(sp, t["w_in"][lay, S_QC + s + 3], S_QC + s + 3)
                sp.wait_ge(row_ready, s + 1)
                sp.dma_start(t["rows"][S_QC + s], row[s % 2][:]).then_inc(stored[s % 2], 16)
            for b in range(2):
                sp.wait_ge(stored[b], 16 * (n_s // 2 + 1))

        @blk.tensor
        def _(pe):
            pe.sem_inc(acc_free, NG)
            with pe.Fori(0, n_s // 2) as i:
                for b in range(2):
                    pe.wait_ge(w.ready, i * 2 + (S_QC + b + 1))
                    project_slice(pe, i * 2 + b, w.parts[b], h, acc, acc_free, acc_ready)

        @blk.gpsimd
        def _(pool):
            zero_pads(pool, row, pads)
            for s in range(2, n_s):
                pool.wait_ge(acc_ready, (s - 1) * NG)
                w.split(pool, S_QC + s, s % 2)

        @blk.scalar
        def _(act):
            for b in range(2):
                act.sem_inc(stored[b], 16)
            act.wait_ge(pads, 6)
            with act.Fori(0, n_s // 2) as i:
                for b in range(2):
                    act.wait_ge(stored[b], 16 * (i + 1))
                    take_out(act, i * 2 + b, acc, acc_ready, acc_free, row[b], ACT.Copy)
                    act.wait_ge(acc_free, (i * 2 + b + 2) * NG)
                    act.sem_inc(row_ready, 1)


def gates_and_rotary(nc, t, lay):
    G = 4 * NH
    with Mem(nc, f"gr{lay}") as m:
        sc = m.sb("sc", TOK)
        ident = m.sb("ident", P)
        dtb, alog, rate = m.sb("dtb", 2, NH), m.sb("alog", 2, NH), m.sb("rate", 2, NH)
        raw, out = m.sb("raw", NT, G), m.sb("out", NT, G)
        z, e, u, ln, pos, w, iszero = (m.sb(n, 2, NT, NH) for n in ("z", "e", "u", "ln", "pos", "w", "iszero"))
        tp = m.ps("tp", NT, G)
        row = [m.sb(f"row{j}", RL) for j in range(4)]
        t1 = [m.sb(f"t1{b}", SEQ) for b in range(2)]
        t2 = [m.sb(f"t2{b}", SEQ) for b in range(2)]
        cos, sin, swap = m.sb("cos", SEQ), m.sb("sin", SEQ), m.sb("swap", P)
        vrow, vt, zero = m.sb("vrow", RL), m.sb("vt", NT, P), m.sb("zero", P)
        ps = m.ps("ps", 4, 512)
        vps = m.ps("vps", 2, 512)
        row_loaded, swap_loaded, turn_loaded = m.sems("row_loaded", 4), m.sem("swap_loaded"), m.sem("turn_loaded")
        v_loaded, zeroed, rows_stored = m.sem("v_loaded"), m.sem("zeroed"), m.sem("rows_stored")
        swapped, cos_done, sin_done, rotated = (m.sem(n) for n in ("swapped", "cos_done", "sin_done", "rotated"))
        v_turned, v_out = m.sem("v_turned"), m.sem("v_out")
        lat = slice(L0, L0 + SEQ)
        NV = (NT + 3) // 4
        loaded, turned, raw_ready = m.sem("loaded"), m.sem("turned"), m.sem("raw_ready")
        act_own, dve_own, stored = m.sem("act_own"), m.sem("dve_own"), m.sem("stored")
        blk = m.block()
        N_DVE = 2 + 4 + 6 + 2

        @blk.sync
        def _(sp):
            src = t["rows"][S_SC, 0:G]
            sp.dma_start(sc[0:G, 0:CTX], src[:, C0:C0 + CTX]).then_inc(loaded, 16)
            sp.dma_start(sc[0:G, CTX:TOK], src[:, L0:L0 + SEQ]).then_inc(loaded, 16)
            sp.dma_start(ident[:], t["ident"]).then_inc(loaded, 16)
            sp.dma_start(dtb[:], t["dt_bias"][lay]).then_inc(loaded, 16)
            sp.dma_start(alog[:], t["a_log"][lay]).then_inc(loaded, 16)
            sp.dma_start(swap[:], t["swap"]).then_inc(swap_loaded, 16)
            sp.dma_start(row[0][:], t["rows"][S_QC]).then_inc(row_loaded[0], 16)
            sp.dma_start(cos[:], t["cos"]).then_inc(turn_loaded, 16)
            sp.dma_start(sin[:], t["sin"]).then_inc(turn_loaded, 16)
            for j in range(1, 4):
                sp.dma_start(row[j][:], t["rows"][S_QC + j]).then_inc(row_loaded[j], 16)
            sp.dma_start(vrow[:], t["rows"][S_VC]).then_inc(v_loaded, 16)
            sp.wait_ge(zeroed, 1)
            sp.dma_start(t["qk"][3, :, TOK:TOK + KPAD], zero[:]).then_inc(rows_stored, 16)
            sp.dma_start(t["vt"][NT], zero[:]).then_inc(rows_stored, 16)
            sp.wait_ge(dve_own, N_DVE)
            sp.wait_ge(act_own, 6)
            sp.dma_start(t["gates"].rearrange("(t p) c -> p t c", p=P), out[:]).then_inc(stored, 16)
            for j in range(4):
                sp.wait_ge(rotated, j + 1)
                for lo, n, col in ((0, CTX, C0), (CTX, SEQ, L0)):
                    sp.dma_start(t["qk"][j, :, lo:lo + n], row[j][:, col:col + n]).then_inc(rows_stored, 16)
            sp.wait_ge(v_out, NV)
            sp.dma_start(t["vt"][0:NT].rearrange("t p c -> p t c"), vt[:]).then_inc(rows_stored, 16)
            sp.wait_ge(stored, 16)
            sp.wait_ge(rows_stored, (2 + 8 + 1) * 16)

        @blk.tensor
        def _(pe):
            pe.wait_ge(loaded, 5 * 16)
            for n in range(NT):
                mm = pe.transpose(tp[:, n, :], sc[0:G, n * P:(n + 1) * P], ident[0:G, 0:G])
            mm.then_inc(turned, 1)
            pe.wait_ge(swap_loaded, 16)
            for j in range(4):
                pe.wait_ge(row_loaded[j], 16)
                for c in range(4):
                    if j > 0:
                        pe.wait_ge(sin_done, (j - 1) * 4 + c + 1)
                    pe.matmul(ps[:, c, :], swap[:], row[j][:, L0 + 512 * c:L0 + 512 * c + 512], start=True, stop=True).then_inc(swapped, 1)
            pe.wait_ge(v_loaded, 16)
            for q in range(NV):
                if q >= 2:
                    pe.wait_ge(v_out, q - 1)
                for n in range(4 * q, min(4 * q + 4, NT)):
                    col = C0 + n * P if n < NCT else L0 + (n - NCT) * P
                    mm = pe.transpose(vps[:, q % 2, (n % 4) * P:(n % 4 + 1) * P], vrow[:, col:col + P], ident[:])
                mm.then_inc(v_turned, 1)

        def part(x, d, kind):
            return x[:, :, (2 * d + kind) * NH:(2 * d + kind + 1) * NH]

        @blk.scalar
        def _(act):
            act.wait_ge(turned, 1)
            act.activation(raw[:], tp[:], ACT.Copy).then_inc(raw_ready, 1)
            s = Steps(act, act_own)
            s.link(act.activation(rate[:], alog[:], ACT.Exp))
            act.wait_ge(dve_own, 2)
            s.link(act.activation(e[:], z[:], ACT.Abs))
            s.link(act.activation(e[:], e[:], ACT.Exp, scale=-1.0))
            act.wait_ge(dve_own, 4)
            s.link(act.activation(ln[:], u[:], ACT.Ln))
            act.wait_ge(raw_ready, 1)
            for d in range(2):
                s.link(act.activation(part(out, d, 0), part(raw, d, 0), ACT.Sigmoid))
            for q in range(NV):
                n = min(4, NT - 4 * q)
                act.wait_ge(v_turned, q + 1)
                act.activation(vt[:, 4 * q:4 * q + n, :], vps[:, q % 2, 0:n * P].rearrange("p (t c) -> p t c", c=P), ACT.Copy).then_inc(v_out, 1)

        @blk.gpsimd
        def _(pool):
            pool.memset(zero[:], 0.0).then_inc(zeroed, 1)
            pool.wait_ge(turn_loaded, 32)
            for j in range(4):
                pool.wait_ge(row_loaded[j], 16)
                if j >= 2:
                    pool.wait_ge(rotated, j - 1)
                pool.tensor_tensor(t1[j % 2][:], row[j][:, lat], cos[:], ALU.mult).then_inc(cos_done, 1)

        @blk.vector
        def _(dve):
            dve.wait_ge(raw_ready, 1)
            s = Steps(dve, dve_own)
            for d in range(2):
                s.link(dve.tensor_tensor(z[:, d], part(raw, d, 1), dtb[:, d:d + 1, :].to_broadcast([P, NT, NH]), ALU.add))
            dve.wait_ge(act_own, 3)
            s.link(dve.tensor_scalar(u[:], e[:], 1.0, None, ALU.add))
            s.link(dve.tensor_scalar(pos[:], z[:], 0.0, None, ALU.max))
            s.link(dve.tensor_scalar(w[:], u[:], -1.0, None, ALU.add))
            s.link(dve.tensor_scalar(iszero[:], w[:], 0.0, None, ALU.is_equal))
            dve.wait_ge(act_own, 4)
            s.link(dve.tensor_tensor(w[:], w[:], iszero[:], ALU.add))
            s.link(dve.tensor_tensor(ln[:], ln[:], iszero[:], ALU.add))
            s.link(dve.reciprocal(w[:], w[:]))
            s.link(dve.tensor_tensor(e[:], e[:], w[:], ALU.mult))
            s.link(dve.tensor_tensor(e[:], e[:], ln[:], ALU.mult))
            s.link(dve.tensor_tensor(pos[:], pos[:], e[:], ALU.add))
            for d in range(2):
                s.link(dve.scalar_tensor_tensor(part(out, d, 1), pos[:, d], -1.0,
                                                rate[:, d:d + 1, :].to_broadcast([P, NT, NH]), ALU.mult, ALU.mult))
            assert s.n == N_DVE, s.n
            dve.wait_ge(turn_loaded, 32)
            for j in range(4):
                for c in range(4):
                    cols = slice(512 * c, 512 * c + 512)
                    dve.wait_ge(swapped, j * 4 + c + 1)
                    dve.tensor_tensor(t2[j % 2][:, cols], ps[:, c, :], sin[:, cols], ALU.mult).then_inc(sin_done, 1)
                dve.wait_ge(sin_done, (j + 1) * 4)
                dve.wait_ge(cos_done, j + 1)
                dve.tensor_tensor(row[j][:, lat], t1[j % 2][:], t2[j % 2][:], ALU.add).then_inc(rotated, 1)


def attention(nc, t, lay, ctx, w_hi=None, w_lo=None):
    nk = NCT if ctx else NCT + 3
    half = nk * P // 2
    n_q = NCT if ctx else SEQ // P
    SC = float(HD) ** -0.5
    with Mem(nc, f"at{lay}{int(ctx)}") as m:
        ident = m.sb("ident", P)
        sink, sink_raw = m.sb("sink", NH), m.sb("sink_raw", NH)
        q = [m.sb(f"q{b}", 3, P) for b in range(2)]
        k = [m.sb(f"k{b}", nk * P) for b in range(2)]
        v = [m.sb(f"v{b}", nk, P) for b in range(2)]
        mask = [m.sb(f"mask{b}", 2 * P) for b in range(2)]
        z = [m.sb(f"z{b}", 3, P) for b in range(2)]
        y = [m.sb(f"y{b}", 3, P) for b in range(2)]
        p = [m.sb(f"p{b}", nk * P) for b in range(3)]
        over_l = [m.sb(f"over_l{b}", P) for b in range(3)]
        pt = [m.sb(f"pt{b}", nk, 3, P) for b in range(2)]
        mx, nb, l, es = (m.sb(n, NH) for n in ("mx", "nb", "l", "es"))
        sps = m.ps("sps", 2, 2, 512)
        tps = m.ps("tps", 2, 512)
        ops = m.ps("ops", 2, 512)
        par_loaded, sink_ready = m.sem("par_loaded"), m.sem("sink_ready")
        loaded, stored = m.sems("loaded", 2), m.sems("stored", 2)
        s_ready, nb_ready, exp_done, p_ready = (m.sem(n) for n in ("s_ready", "nb_ready", "exp_done", "p_ready"))
        t_ready, t_act, o_ready, y_ready = (m.sem(n) for n in ("t_ready", "t_act", "o_ready", "y_ready"))
        dve_own, es_done = m.sem("dve_own"), m.sem("es_done")
        w_raw = None if ctx else m.sb("w_raw", KT, D)
        w_loaded, w_split = m.sem("w_loaded"), m.sem("w_split")
        blk = m.block()
        n_load = 2 if ctx else 9
        split = (nk + 1) // 2

        @blk.sync
        def _(sp):
            sp.dma_start(ident[:], t["ident"]).then_inc(par_loaded, 16)
            sp.dma_start(sink_raw[:], t["sink"][lay]).then_inc(par_loaded, 16)
            for b in range(2):
                sp.sem_inc(stored[b], 16)
                sp.dma_start(k[b][:, (nk - NCT) * P:], t["qk"][3, :, 0:CTX]).then_inc(par_loaded, 16)
                sp.dma_start(v[b][:, nk - NCT:, :], t["vt"][0:NCT].rearrange("t p c -> p t c")).then_inc(par_loaded, 16)

            def load(n, b):
                tok = n * P + (0 if ctx else CTX)
                col = n * P + (C0 if ctx else L0)
                sp.dma_start(q[b][:], t["qk"][0:3, :, bass.ds(tok, P)].rearrange("j p n -> p j n")).then_inc(loaded[b], 16)
                if not ctx:
                    for a, off in enumerate((-1, 1, 0)):
                        sp.dma_start(k[b][:, a * P:(a + 1) * P], t["qk"][3, :, bass.ds(n * P + (CTX + off * P), P)]).then_inc(loaded[b], 16)
                    sp.dma_start(mask[b][:], t["mask"][ds1(n)].rearrange("t p c -> p (t c)")).then_inc(loaded[b], 16)
                    for a, off in enumerate((-1, 1, 0)):
                        sp.dma_start(v[b][:, a:a + 1, :], t["vt"][ds1(n + (NCT + off))].rearrange("t p c -> p t c")).then_inc(loaded[b], 16)
                sp.dma_start(z[b][:], t["rows"][9:12, :, bass.ds(col, P)].rearrange("j p n -> p j n")).then_inc(loaded[b], 16)

            def store(n, b):
                sp.wait_ge(y_ready, 2 * n + 6)
                tok = n * P + (0 if ctx else CTX)
                sp.dma_start(t["yc"][:, :, bass.ds(tok, P)].rearrange("j p n -> p j n"), y[b][:]).then_inc(stored[b], 16)

            for b in range(2):
                load(b, b)
            if not ctx:
                sp.dma_start(w_raw[:], t["w_out"][lay]).then_inc(w_loaded, 16)
            if n_q > 2:
                with sp.Fori(0, n_q // 2 - 1) as i:
                    for b in range(2):
                        sp.wait_ge(y_ready, 4 * i + 2 * b + 6)
                        load(i * 2 + (b + 2), b)
                        store(i * 2 + b, b)
            for b in range(2):
                store(n_q - 2 + b, b)
            for b in range(2):
                sp.wait_ge(stored[b], 16 * (n_q // 2 + 1))

        @blk.tensor
        def _(pe):
            pe.wait_ge(par_loaded, 6 * 16)
            pe.sem_inc(exp_done, 2)
            pe.sem_inc(t_ready, 3)
            pe.sem_inc(t_act, 1)
            pe.sem_inc(o_ready, 4)
            pe.sem_inc(y_ready, 4)

            def scores(n, b, u):
                g, j = divmod(u, 3)
                pe.wait_ge(exp_done, n * NH + u + 1)
                for h in range(2):
                    mm = pe.matmul(sps[:, u % 2, h, 0:half], q[b][g * HD:(g + 1) * HD, j, :],
                                   k[b][g * HD:(g + 1) * HD, h * half:(h + 1) * half], start=True, stop=True)
                mm.then_inc(s_ready, 1)

            def turn(n, u):
                pe.wait_ge(p_ready, n * NH + u + 1)
                pe.wait_ge(t_act, n * NH + u + 1)
                for a in range(nk):
                    h, c = (0, a) if a < split else (1, a - split)
                    mm = pe.matmul(tps[:, h, c * P:(c + 1) * P], p[u % 3][:, a * P:(a + 1) * P], over_l[u % 3][:], start=True, stop=True)
                mm.then_inc(t_ready, 1)

            def values(n, b, g):
                pe.wait_ge(t_act, n * NH + 3 * g + 4)
                pe.wait_ge(y_ready, 2 * n + g + 1)
                for a in range(nk):
                    mm = pe.matmul(ops[g * HD:(g + 1) * HD, b, 0:3 * P], v[b][:, a, g * HD:(g + 1) * HD],
                                   pt[g][:, a, :, :].rearrange("p j n -> p (j n)"), start=(a == 0), stop=(a == nk - 1))
                mm.then_inc(o_ready, 1)

            def tile(n, b, more, turns):
                for u in range(NH - 1):
                    if u + 2 < NH:
                        scores(n, b, u + 2)
                    elif more:
                        pe.wait_ge(loaded[1 - b], 16 * n_load * (turns + b + 1))
                        scores(n + 1, 1 - b, 0)
                    turn(n, u)
                    if u == 3:
                        values(n, b, 0)
                turn(n, NH - 1)
                if more:
                    scores(n + 1, 1 - b, 1)
                values(n, b, 1)

            pe.wait_ge(loaded[0], 16 * n_load)
            scores(0, 0, 0)
            scores(0, 0, 1)
            if n_q > 2:
                with pe.Fori(0, n_q // 2 - 1) as i:
                    for b in range(2):
                        tile(i * 2 + b, b, True, i)
            tile(n_q - 2, 0, True, n_q // 2 - 1)
            tile(n_q - 1, 1, False, None)

        @blk.gpsimd
        def _(pool):
            if not ctx:
                pool.wait_ge(w_loaded, 16)
                for k in range(KT):
                    split_in_two(pool, w_raw[:, k, :], w_hi[:, k, :], w_lo[:, k, :], w_split, k)

        @blk.scalar
        def _(act):
            def exps(n, u):
                act.wait_ge(nb_ready, n * NH + u + 1)
                act.wait_ge(t_ready, n * NH + u + 1)
                act.activation(p[u % 3][:].rearrange("p (h c) -> p h c", h=2), sps[:, u % 2, :, 0:half], ACT.Exp, scale=SC, bias=nb[:, u:u + 1],
                               accum_out=l[:, u:u + 1]).then_inc(exp_done, 1)
                act.activation(es[:, u:u + 1], sink_raw[:, u:u + 1], ACT.Exp, bias=nb[:, u:u + 1]).then_inc(es_done, 1)

            def move(n, u):
                g, j = divmod(u, 3)
                act.wait_ge(t_ready, n * NH + u + 4)
                if j == 0:
                    act.wait_ge(o_ready, 2 * n + g + 3)
                act.activation(pt[g][:, 0:split, j, :], tps[:, 0, 0:split * P].rearrange("p (a n) -> p a n", a=split), ACT.Copy)
                act.activation(pt[g][:, split:nk, j, :], tps[:, 1, 0:(nk - split) * P].rearrange("p (a n) -> p a n", a=nk - split), ACT.Copy).then_inc(t_act, 1)

            act.wait_ge(par_loaded, 6 * 16)

            def tile(n, more):
                for u in range(NH):
                    move(n, u)
                    if u + 2 < NH:
                        exps(n, u + 2)
                    elif more:
                        exps(n + 1, u + 2 - NH)

            exps(0, 0)
            exps(0, 1)
            if n_q > 2:
                with act.Fori(0, n_q // 2 - 1) as i:
                    for b in range(2):
                        tile(i * 2 + b, True)
            tile(n_q - 2, True)
            tile(n_q - 1, False)

        N_OWN = (3 if ctx else 4) * NH
        N_FIRST = (2 if ctx else 4) + 2

        @blk.vector
        def _(dve):
            dve.wait_ge(par_loaded, 6 * 16)
            dve.tensor_scalar(sink[:], sink_raw[:], 1.0 / SC, None, ALU.mult).then_inc(sink_ready, 1)
            dve.wait_ge(sink_ready, 1)

            def highest(s, n, b, u):
                dve.wait_ge(s_ready, n * NH + u + 1)
                if not ctx:
                    s.link(dve.tensor_tensor(sps[:, u % 2, 0, 0:2 * P], sps[:, u % 2, 0, 0:2 * P], mask[b][:], ALU.add))
                s.link(dve.tensor_reduce(mx[:, u:u + 1], sps[:, u % 2, :, 0:half], AX.XY, ALU.max))
                dve.tensor_scalar(nb[:, u:u + 1], mx[:, u:u + 1], sink[:, u:u + 1], -SC, ALU.max, ALU.mult).then_inc(nb_ready, 1)

            def weigh(s, n, u):
                dve.wait_ge(exp_done, n * NH + u + 3)
                dve.wait_ge(es_done, n * NH + u + 1)
                s.link(dve.tensor_tensor(l[:, u:u + 1], l[:, u:u + 1], es[:, u:u + 1], ALU.add))
                s.link(dve.reciprocal(l[:, u:u + 1], l[:, u:u + 1]))
                dve.tensor_scalar(over_l[u % 3][:], ident[:], l[:, u:u + 1], None, ALU.mult).then_inc(p_ready, 1)

            def gated(n, b, g):
                dve.wait_ge(o_ready, 2 * n + g + 5)
                h = slice(g * HD, (g + 1) * HD)
                dve.tensor_tensor(y[b][h], ops[h, b, 0:3 * P].rearrange("p (j n) -> p j n", j=3), z[b][h], ALU.mult).then_inc(y_ready, 1)

            def tile(n, b, more, turns):
                s = Steps(dve, dve_own, n * N_OWN + N_FIRST)
                dve.wait_ge(stored[b], 16 * (turns + 1))
                for u in range(NH):
                    if u + 1 < NH:
                        weigh(s, n, u + 1)
                    elif more:
                        weigh(s, n + 1, 0)
                    if u + 2 < NH:
                        highest(s, n, b, u + 2)
                    elif more:
                        if u + 2 == NH:
                            dve.wait_ge(loaded[1 - b], 16 * n_load * (turns + b + 1))
                        highest(s, n + 1, 1 - b, u + 2 - NH)
                    if u == 4:
                        gated(n, b, 0)
                gated(n, b, 1)
                assert not more or s.n == N_OWN, s.n

            first = Steps(dve, dve_own)
            dve.wait_ge(loaded[0], 16 * n_load)
            highest(first, 0, 0, 0)
            highest(first, 0, 0, 1)
            weigh(first, 0, 0)
            assert first.n == N_FIRST
            if n_q > 2:
                with dve.Fori(0, n_q // 2 - 1) as i:
                    for b in range(2):
                        tile(i * 2 + b, b, True, i)
            tile(n_q - 2, 0, True, n_q // 2 - 1)
            tile(n_q - 1, 1, False, n_q // 2 - 1)


def deltanet(nc, t, lay):
    H = [(h, h // 2, h % 2) for h in range(NH)]
    NL = 6
    GH = NH // 2
    LM_STEP, LT_STEP = 2 * NL, 4 * (NL - 2) + 2
    with Mem(nc, f"dn{lay}") as m:
        ident, blockdiag, tri = m.sb("ident", P), m.sb("blockdiag", P), m.sb("tri", P)
        tri_c, negmask = m.sb("tri_c", CH), m.sb("negmask", CH)
        lmask, umask1, minus_strict = m.sb("lmask", NL, P), m.sb("umask1", P), m.sb("minus_strict", CH)
        dirmask, ones = m.sb("dirmask", 2), m.sb("ones", HD)
        kq = [m.sb(f"kq{b}", NP3, 2, 2, CH) for b in range(2)]
        vf = [m.sb(f"vf{b}", NP3, 2, CH) for b in range(2)]
        gb = [m.sb(f"gb{b}", 2, NH) for b in range(2)]
        gtri = m.sb("gtri", NH, CH)
        gz = m.sb("gz", 2, NP3, 2)
        expo = m.sb("expo", 3, NH)
        ex = [m.sb(f"ex{b}", 3, NH) for b in range(2)]
        bw = [m.sb(f"bw{b}", 2, NH) for b in range(2)]
        xm, dec_in, dec, decb, nbeta = (m.sb(n, NH, CH) for n in ("xm", "dec_in", "dec", "decb", "nbeta"))
        n_c = m.sb("n_c", NH, P)
        at = [m.sb(f"at{b}", NH, CH) for b in range(2)]
        kt = [m.sb(f"kt{b}", NH, CH) for b in range(2)]
        vt = [m.sb(f"vt{b}", NH, CH) for b in range(2)]
        n_t, T, M = m.sb("n_t", NH, P), m.sb("T", NH, P), m.sb("M", NH, P)
        TT = [m.sb(f"TT{b}", NH, P) for b in range(2)]
        state = m.sb("state", NP3, 2, P)
        faded = m.sb("faded", NP3, 2, P)
        kqs = m.sb("kqs", 2, NH, CH)
        rest, v_new, v_dec = m.sb("rest", NH, CH), m.sb("v_new", NH, CH), m.sb("v_dec", NH, CH)
        o = [m.sb(f"o{b}", NH, CH) for b in range(2)]
        p_kq = m.ps("p_kq", 2, 512)
        p_g, p_k, p_v = m.ps("p_g", 512), m.ps("p_k", 512), m.ps("p_v", 512)
        p_l = [m.ps(f"p_l{i}", 512) for i in range(3)]

        par_loaded, loaded, zeroed = m.sem("par_loaded"), m.sems("loaded", 2), m.sem("zeroed")
        gates_ready, sums_done, kv_done, kq_done = (m.sem(n) for n in ("gates_ready", "sums_done", "kv_done", "kq_done"))
        sums_out, expo_ready, ex_ready, bw_ready = (m.sem(n) for n in ("sums_out", "expo_ready", "ex_ready", "bw_ready"))
        xm_ready, dvec_ready, dec_ready, decb_ready = (m.sem(n) for n in ("xm_ready", "dvec_ready", "dec_ready", "decb_ready"))
        nt0_ready = m.sem("nt0_ready")
        kv_out, nc_ready, nt_ready, at_ready, tt0_ready = (m.sem(n) for n in ("kv_out", "nc_ready", "nt_ready", "at_ready", "tt0_ready"))
        lm_done, m_ready, lt_done, t_ready = (m.sem(n) for n in ("lm_done", "m_ready", "lt_done", "t_ready"))
        ks_done, ks_ready, kqs_ready, rest_ready = (m.sem(n) for n in ("ks_done", "ks_ready", "kqs_ready", "rest_ready"))
        tr_done, vn_ready, av_done = (m.sem(n) for n in ("tr_done", "vn_ready", "av_done"))
        faded_ready, state_ready, o_ready = (m.sem(n) for n in ("faded_ready", "state_ready", "o_ready"))
        o_stored, waits_passed = m.sems("o_stored", 2), m.sem("waits_passed")
        blk = m.block()

        def heads(bank):
            return bank[:, 0:NH * CH].rearrange("p (h c) -> p h c", h=NH)

        def col(h):
            return slice(h * CH, (h + 1) * CH)

        DIRS = [(d, slice(d * CH, (d + 1) * CH)) for d in range(2)]
        HALF = [slice(0, HD), slice(HD, P)]

        def group(g):
            return slice(g * GH, (g + 1) * GH)

        def per_head(x):
            return x.unsqueeze(2).to_broadcast([P, NH, CH])

        def all_heads(x):
            return x.unsqueeze(1).to_broadcast([P, NH, CH])

        def plus_one(eng, g):
            return eng.tensor_tensor(n_t[:, group(g), :], n_c[:, group(g), :], ident[:].unsqueeze(1).to_broadcast([P, GH, P]), ALU.add)

        def bank_of(slot):
            return p_l[slot % 3]

        def slot_of(lv, k):
            return 2 + 6 * lv + (k if lv < NL - 2 or k < 2 else k - 2)

        N_LOAD = 8
        N_PAR = 10

        @blk.sync
        def _(sp):
            for dst, n in ((ident, "ident"), (blockdiag, "blockdiag"), (tri, "tri"), (tri_c, "tri_c"), (negmask, "negmask"),
                           (lmask, "lmask"), (umask1, "umask1"), (minus_strict, "minus_strict"),
                           (dirmask, "dirmask"), (ones, "ones")):
                sp.dma_start(dst[:], t[n]).then_inc(par_loaded, 16)

            def load(b, fcol, bcol, ftok, btok):
                for d, (c, tok) in enumerate(((fcol, ftok), (bcol, btok))):
                    sp.dma_start(gb[b][d * CH:(d + 1) * CH], t["gates"][bass.ds(tok, CH), d * 2 * NH:(d + 1) * 2 * NH]
                                 .rearrange("p (k h) -> p k h", k=2)).then_inc(loaded[b], 16)
                for d, (c, tok) in enumerate(((fcol, ftok), (bcol, btok))):
                    for kind in range(3):
                        src = t["rows"][S_QKV + kind:S_QKV + 9:3, :, bass.ds(c, CH)].rearrange("s p c -> p s c")
                        dst = vf[b][:, :, d, :] if kind == 2 else kq[b][:, :, 1 - kind, d, :]
                        sp.dma_start(dst, src).then_inc(loaded[b], 16)

            def store(s, b, ftok, btok):
                sp.wait_ge(o_ready, s + 1)
                for (d, part), tok in zip(DIRS, (ftok, btok)):
                    sp.dma_start(t["scan"][d, bass.ds(tok, CH), :], o[b][part].rearrange("p h c -> p (h c)")).then_inc(o_stored[b], 16)

            def at_step(n):
                if isinstance(n, int) and n < NCSTEP:
                    return (n * CH + C0, (NCSTEP - 1 - n) * CH + C0, n * CH, (NCSTEP - 1 - n) * CH)
                last = NSTEP + NCSTEP - 1
                return (n * CH + (L0 - CTX), n * -CH + (last * CH + L0 - CTX), n * CH, n * -CH + last * CH)

            def turn(n, b):
                sp.wait_ge(ks_done, n)
                load(1 - b, *at_step(n + 1))
                store(n - 1, 1 - b, *at_step(n - 1)[2:])

            for b in range(2):
                sp.sem_inc(o_stored[b], 32)
                load(b, *at_step(b))
            first = (NCSTEP + 2) // 2
            for n in range(1, 2 * first):
                turn(n, n % 2)
            with sp.Fori(first, NSTEP // 2 - 1) as i:
                for b in range(2):
                    turn(i * 2 + b, b)
            turn(NSTEP - 2, 0)
            for s in (NSTEP - 2, NSTEP - 1):
                store(s, s % 2, *at_step(s)[2:])
            for b in range(2):
                sp.wait_ge(o_stored[b], 32 * (NSTEP // 2 + 1))

        @blk.tensor
        def _(pe):
            pe.wait_ge(par_loaded, N_PAR * 16)

            def wait_apart(sem, value):
                pe.wait_ge(sem, value)
                pe.sem_inc(waits_passed, 1)

            def known(n, low):
                return not isinstance(n, int) or n > low

            def decay_sums(c, b, i):
                wait_apart(loaded[b], 16 * N_LOAD * (i + 1))
                wait_apart(gates_ready, c + 1)
                if known(c, 1):
                    wait_apart(state_ready, c)
                elif c == 1:
                    pe.wait_ge(dvec_ready, 1)
                g = gb[b][:, 1, :]
                pe.matmul(p_g[:, 384:390], tri[:], g, start=True, stop=True)
                pe.matmul(p_g[:, 390:396], blockdiag[:], g, start=True, stop=True)
                for hh in range(2):
                    pe.matmul(p_g[HALF[hh], 396:402], ones[:], gz[:, hh].rearrange("p a d -> p (a d)"), start=True, stop=True)
                pe.matmul(p_g[:, 0:384], blockdiag[:], gtri[:].rearrange("p h c -> p (h c)"), start=True, stop=True).then_inc(sums_done, 1)

            def chunk_products(c, b):
                if known(c, 1):
                    wait_apart(kqs_ready, c - 1)
                elif c == 1:
                    pe.wait_ge(at_ready, 1)
                for h, pair, hh in H:
                    for d, part in DIRS:
                        mm = pe.matmul(p_kq[part, hh, pair * P:(pair + 1) * P], kq[b][HALF[hh], pair, 0, d, :],
                                       kq[b][HALF[hh], pair, :, d, :], start=True, stop=True)
                mm.then_inc(kq_done, 1)

            def turn_kv(c, b):
                if known(c, 1):
                    wait_apart(o_ready, c - 1)
                    wait_apart(state_ready, c)
                elif c == 1:
                    pe.wait_ge(kv_out, 1)
                for pair in range(NP3):
                    pe.transpose(p_k[:, pair * P:(pair + 1) * P], kq[b][:, pair, 0].rearrange("p d c -> p (d c)"), ident[:])
                for pair in range(NP3):
                    mm = pe.transpose(p_v[:, pair * P:(pair + 1) * P], vf[b][:, pair].rearrange("p d c -> p (d c)"), ident[:])
                mm.then_inc(kv_done, 1)

            def s_products(s, B):
                wait_apart(at_ready, s + 2)
                wait_apart(state_ready, s + 1)
                for pair in range(NP3):
                    for d, part in DIRS:
                        for k in range(2):
                            mm = pe.matmul(p_kq[part, k, pair * P:(pair + 1) * P], kq[B][:, pair, k, d, :],
                                           state[:, pair, d, :], start=True, stop=True)
                mm.then_inc(ks_done, 1)

            def t_products(s, B):
                wait_apart(rest_ready, s + 1)
                for h in range(NH):
                    for d, part in DIRS:
                        mm = pe.matmul(p_g[part, col(h)], TT[B][part, h, part], rest[part, h, :], start=True, stop=True)
                mm.then_inc(tr_done, 1)

            def v_products(s, B):
                wait_apart(vn_ready, s + 1)
                for h in range(NH):
                    for d, part in DIRS:
                        pe.matmul(p_k[part, col(h)], at[B][part, h, :], v_new[part, h, :], start=True, stop=True)
                for h, pair, hh in H:
                    for d, part in DIRS:
                        mm = pe.matmul((p_v, p_g)[d][HALF[hh], pair * CH:(pair + 1) * CH], kt[B][part, h, :], v_dec[part, h, :], start=True, stop=True)
                mm.then_inc(av_done, 1)

            def square(slot, g, lhs, rhs):
                for j in range(GH):
                    h = g * GH + j
                    mm = pe.matmul(bank_of(slot)[:, j * P:(j + 1) * P], lhs[:, h, :], rhs[:, h, :], start=True, stop=True)
                return mm

            def step(n, b, scan, prep, i):
                B = 1 - b
                pe.wait_ge(nt0_ready, n + 1)
                turned(0, 0)
                pe.wait_ge(nt_ready, n + 1)
                if known(n, 0):
                    pe.wait_ge(t_ready, n * LT_STEP - 1)
                turned(1, 1)
                for lv in range(NL - 1):
                    m_at, t_at = n * LM_STEP + 2 + 2 * lv, n * LT_STEP + 4 * lv
                    if lv == 0:
                        pe.wait_ge(m_ready, m_at - 1)
                        if known(n, 0):
                            pe.wait_ge(t_ready, t_at)
                    else:
                        pe.wait_ge(t_ready, t_at - 2)
                    square(slot_of(lv, 0), 0, n_t, T).then_inc(lm_done, 1)
                    pe.wait_ge(*((m_ready, m_at) if lv == 0 else (t_ready, t_at - 1)))
                    square(slot_of(lv, 1), 1, n_t, T).then_inc(lm_done, 1)
                    if scan and lv == 0:
                        s_products(n - 1, B)
                    if scan and lv == 1:
                        t_products(n - 1, B)
                    if scan and lv == 2:
                        v_products(n - 1, B)
                    if prep and lv == 3:
                        decay_sums(n + 1, B, i)
                        chunk_products(n + 1, B)
                    if prep and lv == 4:
                        turn_kv(n + 1, B)
                    if lv == 0:
                        pe.wait_ge(tt0_ready, n + 1)
                    else:
                        pe.wait_ge(t_ready, t_at)
                    last = lv == NL - 2
                    for g in range(2):
                        pe.wait_ge(m_ready, m_at + 1 + g)
                        if not last:
                            square(slot_of(lv, 2 + g), g, TT[b], M).then_inc(lt_done, 1)
                        else:
                            square(slot_of(lv, 4 + g), g, M, TT[b]).then_inc(lt_done, 1)
                    if not last:
                        square(slot_of(lv, 4), 0, M, TT[b]).then_inc(lt_done, 1)
                        pe.wait_ge(t_ready, t_at + 1)
                        square(slot_of(lv, 5), 1, M, TT[b]).then_inc(lt_done, 1)

            def turned(slot, g):
                for j in range(GH):
                    mm = pe.matmul(bank_of(slot)[:, j * P:(j + 1) * P], n_t[:, g * GH + j, :], ident[:], start=True, stop=True)
                mm.then_inc(lm_done, 1)

            decay_sums(0, 0, 0)
            chunk_products(0, 0)
            turn_kv(0, 0)
            step(0, 0, False, True, 0)
            step(1, 1, True, True, 1)
            with pe.Fori(1, NSTEP // 2 - 1) as i:
                for b in range(2):
                    step(i * 2 + b, b, True, True, i + b)
            step(NSTEP - 2, 0, True, True, NSTEP // 2 - 1)
            step(NSTEP - 1, 1, True, False, None)
            s = NSTEP - 1
            pe.wait_ge(state_ready, s + 1)
            for pair in range(NP3):
                for d, part in DIRS:
                    for k in range(2):
                        mm = pe.matmul(p_kq[part, k, pair * P:(pair + 1) * P], kq[1][:, pair, k, d, :],
                                       state[:, pair, d, :], start=True, stop=True)
            mm.then_inc(ks_done, 1)
            pe.wait_ge(t_ready, NSTEP * LT_STEP)
            t_products(s, 1)
            v_products(s, 1)

        @blk.scalar
        def _(act):
            act.wait_ge(par_loaded, N_PAR * 16)

            def sums(c):
                act.wait_ge(sums_done, c + 1)
                act.activation(expo[:], p_g[:, 384:402].rearrange("p (k h) -> p k h", k=3), ACT.Copy).then_inc(sums_out, 1)

            def decays(c):
                act.wait_ge(dvec_ready, c + 1)
                if not (isinstance(c, int) and c == 0):
                    act.wait_ge(at_ready, c)
                act.activation(dec[:], dec_in[:], ACT.Exp).then_inc(dec_ready, 1)

            def exps(c, b):
                act.wait_ge(expo_ready, c + 1)
                act.activation(ex[b][:], expo[:], ACT.Exp).then_inc(ex_ready, 1)

            def kv(c, b):
                act.wait_ge(kv_done, c + 1)
                act.activation(kt[b][:], heads(p_k), ACT.Copy)
                act.activation(vt[b][:], heads(p_v), ACT.Copy).then_inc(kv_out, 1)

            def take(n, lv, k, dst, g):
                last = lv == NL - 2
                act.wait_ge(lt_done, n * LT_STEP + 4 * lv + (k - 3 if last else k - 1))
                act.activation(dst[:, group(g), :], bank_of(slot_of(lv, k))[:, 0:GH * P].rearrange("p (h c) -> p h c", h=GH), ACT.Copy).then_inc(t_ready, 1)

            def step(n, b, prep):
                for lv in range(NL - 1):
                    if prep and lv == 3:
                        sums(n + 1)
                        decays(n + 1)
                    if lv < NL - 2:
                        take(n, lv, 2, T, 0)
                        take(n, lv, 3, T, 1)
                        if prep and lv == 3:
                            exps(n + 1, 1 - b)
                    elif prep:
                        kv(n + 1, 1 - b)
                    take(n, lv, 4, TT[b], 0)
                    take(n, lv, 5, TT[b], 1)

            sums(0)
            decays(0)
            exps(0, 0)
            kv(0, 0)
            step(0, 0, True)
            step(1, 1, True)
            with act.Fori(1, NSTEP // 2 - 1) as i:
                for b in range(2):
                    step(i * 2 + b, b, True)
            step(NSTEP - 2, 0, True)
            step(NSTEP - 1, 1, False)

        @blk.gpsimd
        def _(pool):
            pool.wait_ge(par_loaded, N_PAR * 16)

            def fade(s, b):
                pool.wait_ge(state_ready, s + 1)
                pool.tensor_tensor(faded[:].rearrange("p a d c -> p (a d) c"), state[:].rearrange("p a d c -> p (a d) c"),
                                   ex[b][:, 2, :].unsqueeze(2).to_broadcast([P, NH, P]), ALU.mult).then_inc(faded_ready, 1)

            def prepare(c, b, i):
                first = isinstance(c, int) and c == 0
                pool.wait_ge(loaded[b], 16 * N_LOAD * (i + 1))
                if not first:
                    pool.wait_ge(sums_done, c)
                g, beta = gb[b][:, 1, :], gb[b][:, 0, :]
                pool.tensor_tensor(gtri[:], all_heads(tri_c[:]), per_head(g), ALU.mult)
                g4 = g.rearrange("p (a h) -> p h a", h=2)
                for hh in range(2):
                    ins = pool.tensor_tensor(gz[:, hh], g4[:, hh, :].unsqueeze(2).to_broadcast([P, NP3, 2]),
                                             dirmask[:].unsqueeze(1).to_broadcast([P, NP3, 2]), ALU.mult)
                ins.then_inc(gates_ready, 1)
                pool.tensor_tensor(nbeta[:], all_heads(minus_strict[:]), per_head(beta), ALU.mult)
                pool.wait_ge(sums_out, c + 1)
                if not first:
                    pool.wait_ge(dvec_ready, c)
                pool.tensor_tensor(xm[:], all_heads(negmask[:]), per_head(expo[:, 0, :]), ALU.subtract).then_inc(xm_ready, 1)
                pool.tensor_tensor(expo[:, 1, :], expo[:, 1, :], expo[:, 0, :], ALU.subtract).then_inc(expo_ready, 1)
                pool.wait_ge(dec_ready, c + 1)
                pool.tensor_tensor(decb[:], dec[:], nbeta[:], ALU.mult).then_inc(decb_ready, 1)
                pool.wait_ge(ex_ready, c + 1)
                pool.tensor_tensor(bw[b][:, 1, :], beta, ex[b][:, 1, :], ALU.mult)
                pool.tensor_copy(bw[b][:, 0, :], beta).then_inc(bw_ready, 1)
                pool.wait_ge(nc_ready, c + 1)
                if not first:
                    pool.wait_ge(lm_done, c * LM_STEP)
                plus_one(pool, 1).then_inc(nt_ready, 1)
                pool.wait_ge(nt_ready, c + 1)
                pool.wait_ge(nt0_ready, c + 1)
                pool.tensor_tensor(TT[b][:], n_t[:], umask1[:].unsqueeze(1).to_broadcast([P, NH, P]), ALU.mult).then_inc(tt0_ready, 1)

            prepare(0, 0, 0)
            prepare(1, 1, 0)
            fade(0, 0)
            prepare(2, 0, 1)
            with pool.Fori(1, NSTEP // 2 - 1) as i:
                for b in range(2):
                    n = i * 2 + b
                    fade(n - 1, 1 - b)
                    prepare(n + 1, 1 - b, i + b)
            fade(NSTEP - 3, 1)
            prepare(NSTEP - 1, 1, NSTEP // 2 - 1)
            fade(NSTEP - 2, 0)
            fade(NSTEP - 1, 1)

        @blk.vector
        def _(dve):
            dve.memset(n_c[:], 0.0).then_inc(zeroed, 1)
            dve.memset(state[:], 0.0).then_inc(state_ready, 1)
            dve.wait_ge(zeroed, 1)
            dve.wait_ge(par_loaded, N_PAR * 16)

            def kq_bank(k):
                return p_kq[:, :, 0:3 * P].rearrange("p h (a k c) -> p h a k c", a=NP3, k=2)[:, :, :, k, :]

            def split(x):
                return x.rearrange("p (a h) c -> p h a c", h=2)

            def decay_exponents(c):
                dve.wait_ge(xm_ready, c + 1)
                dve.tensor_tensor(dec_in[:], heads(p_g), xm[:], ALU.add).then_inc(dvec_ready, 1)

            def chunk_matrices(c, b):
                dve.wait_ge(kq_done, c + 1)
                dve.wait_ge(decb_ready, c + 1)
                for d, part in DIRS:
                    ins = dve.tensor_tensor(split(n_c[part, :, part]), kq_bank(0)[part], split(decb[part]), ALU.mult)
                ins.then_inc(nc_ready, 1)
                dve.wait_ge(nc_ready, c + 1)
                if not (isinstance(c, int) and c == 0):
                    dve.wait_ge(lm_done, c * LM_STEP)
                plus_one(dve, 0).then_inc(nt0_ready, 1)
                dve.tensor_tensor(split(at[b][:]), kq_bank(1), split(dec[:]), ALU.mult).then_inc(at_ready, 1)

            def mask(n, slot, at_count, dst, lv, g):
                dve.wait_ge(lm_done, n * LM_STEP + at_count)
                dve.tensor_tensor(dst[:, group(g), :], bank_of(slot)[:, 0:GH * P].rearrange("p (h c) -> p h c", h=GH),
                                  lmask[:, lv, :].unsqueeze(1).to_broadcast([P, GH, P]), ALU.mult).then_inc(m_ready, 1)

            def step(n, b, scan, prep, i):
                B = 1 - b
                for g in range(2):
                    mask(n, g, 1 + g, T, 0, g)
                for lv in range(NL - 1):
                    for g in range(2):
                        mask(n, slot_of(lv, g), 3 + 2 * lv + g, M, lv + 1, g)
                    if scan and lv == 0:
                        scan_front(n - 1, B)
                    if scan and lv == 1:
                        scan_values(n - 1, B)
                    if scan and lv == 2:
                        scan_end(n - 1, B, i)
                    if prep and lv == 3:
                        decay_exponents(n + 1)
                    if prep and lv == 4:
                        chunk_matrices(n + 1, B)

            def scan_front(s, b):
                dve.wait_ge(ks_done, s + 1)
                dve.wait_ge(ex_ready, s + 1)
                for k, sem in enumerate((ks_ready, kqs_ready)):
                    dve.tensor_tensor(kqs[:, k], heads(p_kq[:, k]), per_head(ex[b][:, 0, :]), ALU.mult).then_inc(sem, 1)
                dve.wait_ge(ks_ready, s + 1)
                dve.wait_ge(kv_out, s + 1)
                dve.tensor_tensor(rest[:], vt[b][:], kqs[:, 0], ALU.subtract).then_inc(rest_ready, 1)

            def scan_values(s, b):
                dve.wait_ge(tr_done, s + 1)
                dve.wait_ge(bw_ready, s + 1)
                dve.tensor_tensor(v_new[:], heads(p_g), per_head(bw[b][:, 0, :]), ALU.mult)
                dve.tensor_tensor(v_dec[:], heads(p_g), per_head(bw[b][:, 1, :]), ALU.mult).then_inc(vn_ready, 1)

            def scan_end(s, b, before):
                dve.wait_ge(av_done, s + 1)
                dve.wait_ge(faded_ready, s + 1)
                for d, bank in enumerate((p_v, p_g)):
                    for part in HALF:
                        ins = dve.tensor_tensor(state[part, :, d, part], faded[part, :, d, part],
                                                bank[part, 0:NP3 * CH].rearrange("p (a c) -> p a c", a=NP3), ALU.add)
                ins.then_inc(state_ready, 1)
                dve.wait_ge(kqs_ready, s + 1)
                dve.wait_ge(o_stored[b], before * 32 + 32)
                dve.tensor_tensor(o[b][:], kqs[:, 1], heads(p_k), ALU.add).then_inc(o_ready, 1)

            decay_exponents(0)
            chunk_matrices(0, 0)
            step(0, 0, False, True, None)
            step(1, 1, True, True, 0)
            with dve.Fori(1, NSTEP // 2 - 1) as i:
                step(i * 2, 0, True, True, i - 1)
                step(i * 2 + 1, 1, True, True, i)
            step(NSTEP - 2, 0, True, True, NSTEP // 2 - 2)
            step(NSTEP - 1, 1, True, False, NSTEP // 2 - 1)
            s = NSTEP - 1
            scan_front(s, 1)
            scan_values(s, 1)
            scan_end(s, 1, NSTEP // 2 - 1)


def finish(nc, t, lay, w_hi, w_lo):
    last = lay == DEPTH - 1
    first = NCT if last else 0
    n_t = NT - first
    with Mem(nc, f"fin{lay}") as m:
        ident, mean_w = m.sb("ident", P), m.sb("mean_w", P)
        gate = m.sb("gate", 2, D)
        fnw, ln_w, ln_b, dn_w, eps = m.sb("fnw", D), m.sb("ln_w", 2), m.sb("ln_b", 2), m.sb("dn_w", 1), m.sb("eps", 1)
        u = [m.sb(f"u{b}", 2, P) for b in range(2)]
        za = [m.sb(f"za{b}", 2, P) for b in range(2)]
        zb = [m.sb(f"zb{b}", 3, P) for b in range(2)]
        of = [m.sb(f"of{b}", NH, HD) for b in range(2)]
        ob = [m.sb(f"ob{b}", NH, HD) for b in range(2)]
        x = [m.sb(f"x{b}", D) for b in range(2)]
        y = [m.sb(f"y{b}", KT, P) for b in range(2)]
        y_hi, y_lo = ([m.sb_r(f"{n}{b}", KT, P) for b in range(2)] for n in ("y_hi", "y_lo"))
        usq, sd, rs, osq = m.sb("usq", 2, P), m.sb("sd", P), m.sb("rs", P), m.sb("osq", NH, HD)
        oss, orms, orn = m.sb("oss", NH), m.sb("orms", NH), m.sb("orn", NH)
        gy = m.sb("gy", D)
        xo = [m.sb(f"xo{b}", D) for b in range(2)]
        xss, xrms, xrn, sq = m.sb("xss", 1), m.sb("xrms", 1), m.sb("xrn", 1), m.sb("sq", D)
        res = [m.sb(f"res{b}", D) for b in range(2)]
        mps = m.ps("mps", 2, 512)
        tps = m.ps("tps", 512)
        ops = m.ps("ops", 2, 2, 512)
        par_loaded, eps_ready = m.sem("par_loaded"), m.sem("eps_ready")
        loaded, late_loaded, stored = m.sems("loaded", 2), m.sems("late_loaded", 2), m.sems("stored", 2)
        gate_loaded = m.sem("gate_loaded")
        mean_done, var_done, turned, out_done = (m.sem(n) for n in ("mean_done", "var_done", "turned", "out_done"))
        centred, usq_ready, rs_ready, un_ready, silu_ready, ya_ready = (m.sem(n) for n in ("centred", "usq_ready", "rs_ready", "un_ready", "silu_ready", "ya_ready"))
        o_ready, osq_ready, oss_ready, orn_ready, on_ready, yb_ready = (m.sem(n) for n in ("o_ready", "osq_ready", "oss_ready", "orn_ready", "on_ready", "yb_ready"))
        gy_ready, xo_ready, xr_ready, res_ready = (m.sem(n) for n in ("gy_ready", "xo_ready", "xr_ready", "res_ready"))
        sd_ready, orms_ready, xss_ready, xrms_ready = (m.sem(n) for n in ("sd_ready", "orms_ready", "xss_ready", "xrms_ready"))
        bc_hi, bc_lo, a_hi, a_lo = (m.sem(n) for n in ("bc_hi", "bc_lo", "a_hi", "a_lo"))
        blk = m.block()
        rows = t["rows"]
        N_LOAD, N_LATE = 7, 1
        x_src = t["x_in"] if lay == 0 else t["x_mid"]

        @blk.sync
        def _(sp):
            for dst, n in ((ident, "ident"), (mean_w, "mean_w"), (fnw, "fnw")):
                sp.dma_start(dst[:], t[n]).then_inc(par_loaded, 16)
            for dst, n in ((ln_w, "ln_w"), (ln_b, "ln_b"), (dn_w, "dn_w")):
                sp.dma_start(dst[:], t[n][lay]).then_inc(par_loaded, 16)

            def load(m, b, off):
                tok = m * P + first * P
                for d, dst in enumerate((of, ob)):
                    sp.dma_start(dst[b][:].rearrange("p h c -> p (h c)"), t["scan"][d, bass.ds(tok, P), :]).then_inc(loaded[b], 16)
                for dst, src in ((u[b][:], rows[A_CONV[0]:A_CONV[1] + 1:6]), (za[b][:], rows[Z_SLICE[0]:Z_SLICE[1] + 1]),
                                 (zb[b][:, 0:2, :], rows[4:6]), (zb[b][:, 2:3, :], rows[8:9])):
                    sp.dma_start(dst, src[:, :, bass.ds(tok + off, P)].rearrange("s p n -> p s n")).then_inc(loaded[b], 16)
                sp.dma_start(y[b][:, 5:8, :], t["yc"][:, :, bass.ds(tok, P)].rearrange("s p n -> p s n")).then_inc(loaded[b], 16)

            def load_late(m, b):
                tok = m * P + first * P
                sp.dma_start(x[b][:], x_src[bass.ds(tok, P), :]).then_inc(late_loaded[b], 16)

            def store(m, b):
                tok = m * P + first * P
                if last:
                    sp.dma_start(t["out"][bass.ds(m * P, P), :], res[b][:]).then_inc(stored[b], 16)
                else:
                    sp.dma_start(t["x_mid"][bass.ds(tok, P), :], xo[b][:]).then_inc(stored[b], 16)

            def turn(m, b, early=True, late=True, before=True):
                if early:
                    sp.wait_ge(a_lo, m + 1)
                    load(m + 2, b, L0 - CTX)
                if before:
                    sp.wait_ge(*((res_ready, m) if last else (xo_ready, 2 * m)))
                    store(m - 1, 1 - b)
                    if late:
                        load_late(m + 1, 1 - b)

            for b in range(2):
                sp.sem_inc(stored[b], 16)
                load(b, b, L0 - CTX if last else C0)
            for c in range(2):
                for a in range(2):
                    sp.dma_start(gate[:, c, 512 * a:512 * a + 512], t["mod"][6 * lay + 4 + a, c].partition_broadcast(P)).then_inc(gate_loaded, 16)
            for b in range(2):
                load_late(b, b)
            turn(0, 0, before=False)
            turn(1, 1)
            with sp.Fori(1, n_t // 2 - 1) as i:
                for b in range(2):
                    turn(i * 2 + b, b)
            turn(n_t - 2, 0, early=False)
            turn(n_t - 1, 1, early=False, late=False)
            turn(n_t, 0, early=False, late=False)
            for b in range(2):
                sp.wait_ge(stored[b], 16 * (n_t // 2 + 1))

        @blk.tensor
        def _(pe):
            pe.wait_ge(par_loaded, 6 * 16)

            def project(m, b, h, ks):
                if h == 0 and ks[0] == 0:
                    pe.wait_ge(bc_lo, m + 1)
                    pe.wait_ge(a_lo, m + 1)
                cols = slice(512 * h, 512 * h + 512)
                mm = in_parts(pe, ops[:, b, h, :], lambda k: (y_hi[b][:, k, :], y_lo[b][:, k, :]), lambda k: (w_hi[:, k, cols], w_lo[:, k, cols]), ks)
                if ks[-1] == KT - 1:
                    mm.then_inc(out_done, 1)

            def turn(m, b, i, before=True, this=True):
                if this:
                    pe.wait_ge(loaded[b], 16 * N_LOAD * (i + 1))
                    for c in range(2):
                        mm = pe.matmul(mps[:, 0, 0:P], mean_w[:], u[b][:, c, :], start=(c == 0), stop=(c == 1))
                    mm.then_inc(mean_done, 1)
                if before:
                    project(m - 1, 1 - b, 0, range(KT // 2))
                if this:
                    pe.wait_ge(usq_ready, m + 1)
                    if before:
                        pe.wait_ge(rs_ready, m)
                    for c in range(2):
                        mm = pe.matmul(mps[:, 1, 0:P], mean_w[:], usq[:, c, :], start=(c == 0), stop=(c == 1))
                    mm.then_inc(var_done, 1)
                    pe.wait_ge(on_ready, m + 1)
                    for pair in range(NP3):
                        mm = pe.transpose(tps[:, pair * P:(pair + 1) * P], of[b][:, 2 * pair:2 * pair + 2, :].rearrange("p h c -> p (h c)"), ident[:])
                    mm.then_inc(turned, 1)
                if before:
                    project(m - 1, 1 - b, 0, range(KT // 2, KT))
                    project(m - 1, 1 - b, 1, range(KT))

            turn(0, 0, 0, before=False)
            turn(1, 1, 0)
            with pe.Fori(1, n_t // 2) as i:
                for b in range(2):
                    turn(i * 2 + b, b, i)
            turn(n_t, 0, n_t // 2, this=False)

        @blk.scalar
        def _(act):
            act.wait_ge(par_loaded, 6 * 16)
            act.wait_ge(eps_ready, 1)

            def head_norms(m):
                act.wait_ge(oss_ready, m + 1)
                act.activation(orms[:], oss[:], ACT.Sqrt, scale=1.0 / HD, bias=eps[:]).then_inc(orms_ready, 1)

            def final(m, b):
                act.wait_ge(xo_ready, 2 * m + 2)
                act.activation(sq[:], xo[b][:], ACT.Square, accum_out=xss[:]).then_inc(xss_ready, 1)
                act.wait_ge(xss_ready, m + 1)
                if not (isinstance(m, int) and m == 0):
                    act.wait_ge(xr_ready, m)
                act.activation(xrms[:], xss[:], ACT.Sqrt, scale=1.0 / D, bias=eps[:]).then_inc(xrms_ready, 1)

            def turn(m, b, i, ahead=True):
                if last and not (isinstance(m, int) and m < 2):
                    final(m - 2, b)
                act.wait_ge(var_done, m + 1)
                if not (isinstance(m, int) and m == 0):
                    act.wait_ge(rs_ready, m)
                act.activation(sd[:], mps[:, 1, 0:P], ACT.Sqrt, bias=eps[:]).then_inc(sd_ready, 1)
                act.wait_ge(loaded[b], 16 * N_LOAD * (i + 1))
                act.wait_ge(yb_ready, m + 1)
                act.activation(y_hi[b][:, 2:8, :], y[b][:, 2:8, :], ACT.Copy).then_inc(bc_hi, 1)
                act.wait_ge(un_ready, m + 1)
                for c in range(2):
                    ins = act.activation(u[b][:, c, :], u[b][:, c, :], ACT.Silu, scale=ln_w[:, c:c + 1], bias=ln_b[:, c:c + 1])
                ins.then_inc(silu_ready, 1)
                act.wait_ge(ya_ready, m + 1)
                act.activation(y_hi[b][:, 0:2, :], y[b][:, 0:2, :], ACT.Copy).then_inc(a_hi, 1)
                if ahead:
                    head_norms(m + 1)

            head_norms(0)
            turn(0, 0, 0)
            turn(1, 1, 0)
            with act.Fori(1, n_t // 2 - 1) as i:
                for b in range(2):
                    turn(i * 2 + b, b, i)
            turn(n_t - 2, 0, n_t // 2 - 1)
            turn(n_t - 1, 1, n_t // 2 - 1, ahead=False)
            if last:
                final(n_t - 2, 0)
                final(n_t - 1, 1)

        @blk.gpsimd
        def _(pool):
            def head_squares(m, b):
                pool.wait_ge(o_ready, m + 1)
                pool.tensor_tensor(osq[:], of[b][:], of[b][:], ALU.mult).then_inc(osq_ready, 1)

            def turn(m, b, ahead=True):
                pool.wait_ge(centred, m + 1)
                pool.tensor_tensor(usq[:], u[b][:], u[b][:], ALU.mult).then_inc(usq_ready, 1)
                pool.wait_ge(bc_hi, m + 1)
                pool.tensor_tensor(y_lo[b][:, 2:8, :], y[b][:, 2:8, :], y_hi[b][:, 2:8, :].bitcast(F32), ALU.subtract).then_inc(bc_lo, 1)
                pool.wait_ge(silu_ready, m + 1)
                pool.tensor_tensor(y[b][:, 0:2, :], u[b][:], za[b][:], ALU.mult).then_inc(ya_ready, 1)
                pool.wait_ge(a_hi, m + 1)
                pool.tensor_tensor(y_lo[b][:, 0:2, :], y[b][:, 0:2, :], y_hi[b][:, 0:2, :].bitcast(F32), ALU.subtract).then_inc(a_lo, 1)
                if ahead:
                    head_squares(m + 1, 1 - b)

            head_squares(0, 0)
            with pool.Fori(0, n_t // 2 - 1) as i:
                for b in range(2):
                    turn(i * 2 + b, b)
            turn(n_t - 2, 0)
            turn(n_t - 1, 1, ahead=False)

        @blk.vector
        def _(dve):
            dve.memset(eps[:], EPS).then_inc(eps_ready, 1)
            dve.wait_ge(par_loaded, 6 * 16)

            def gated(m, b, h, c, turns):
                cols = slice(512 * h, 512 * h + 512)
                dve.wait_ge(out_done, 2 * m + h + 1)
                dve.tensor_tensor(gy[:, cols], ops[:, b, h, :], gate[:, c, cols], ALU.mult).then_inc(gy_ready, 1)
                dve.wait_ge(gy_ready, 2 * m + h + 1)
                if h == 0:
                    dve.wait_ge(late_loaded[b], 16 * N_LATE * (turns + 1))
                    dve.wait_ge(stored[b], 16 * (turns + 1))
                dve.tensor_tensor(xo[b][:, cols], gy[:, cols], x[b][:, cols], ALU.add).then_inc(xo_ready, 1)

            def scaled(m, b, turns):
                dve.wait_ge(xrms_ready, m + 1)
                dve.reciprocal(xrn[:], xrms[:]).then_inc(xr_ready, 1)
                dve.wait_ge(xr_ready, m + 1)
                dve.wait_ge(stored[b], 16 * (turns + 1))
                dve.scalar_tensor_tensor(res[b][:], xo[b][:], xrn[:], fnw[:], ALU.mult, ALU.mult).then_inc(res_ready, 1)

            def head_norms(m, b, i):
                dve.wait_ge(loaded[b], 16 * N_LOAD * (i + 1))
                dve.tensor_tensor(of[b][:], of[b][:], ob[b][:], ALU.add).then_inc(o_ready, 1)
                dve.wait_ge(osq_ready, m + 1)
                dve.tensor_reduce(oss[:], osq[:], AX.X, ALU.add).then_inc(oss_ready, 1)
                dve.wait_ge(orms_ready, m + 1)
                dve.reciprocal(orn[:], orms[:]).then_inc(orn_ready, 1)
                dve.wait_ge(orn_ready, m + 1)
                dve.tensor_tensor(of[b][:], of[b][:], orn[:].unsqueeze(2).to_broadcast([P, NH, HD]), ALU.mult).then_inc(on_ready, 1)

            def ends(m, b, i, c):
                gated(m - 2, b, 1, c, None)
                if last:
                    scaled(m - 2, b, i - 1)

            def turn(m, b, i, c2=0, c1=0, ahead=True):
                started = lambda k: not isinstance(m, int) or m >= k
                if started(2):
                    gated(m - 2, b, 1, c2, None)
                dve.wait_ge(mean_done, m + 1)
                dve.tensor_tensor(u[b][:], u[b][:], mps[:, 0:1, 0:P].to_broadcast([P, 2, P]), ALU.subtract).then_inc(centred, 1)
                if last and started(2):
                    scaled(m - 2, b, i - 1)
                dve.wait_ge(turned, m + 1)
                dve.scalar_tensor_tensor(y[b][:, 2:5, :], tps[:, 0:3 * P].rearrange("p (s n) -> p s n", s=3), dn_w[:], zb[b][:],
                                         ALU.mult, ALU.mult).then_inc(yb_ready, 1)
                dve.wait_ge(sd_ready, m + 1)
                dve.reciprocal(rs[:], sd[:]).then_inc(rs_ready, 1)
                dve.wait_ge(rs_ready, m + 1)
                dve.tensor_tensor(u[b][:], u[b][:], rs[:].unsqueeze(1).to_broadcast([P, 2, P]), ALU.mult).then_inc(un_ready, 1)
                if started(1):
                    gated(m - 1, 1 - b, 0, c1, i - 1 + b)
                if ahead:
                    head_norms(m + 1, 1 - b, i + b)

            ctx = 0 if last else 1
            head_norms(0, 0, 0)
            turn(0, 0, 0)
            dve.wait_ge(gate_loaded, 4 * 16)
            turn(1, 1, 0, 0, ctx)
            turn(2, 0, 1, ctx, ctx)
            turn(3, 1, 1, ctx, 0)
            with dve.Fori(2, n_t // 2 - 1) as i:
                for b in range(2):
                    turn(i * 2 + b, b, i)
            turn(n_t - 2, 0, n_t // 2 - 1)
            turn(n_t - 1, 1, n_t // 2 - 1, ahead=False)
            ends(n_t, 0, n_t // 2, 0)
            gated(n_t - 1, 1, 0, 0, n_t // 2 - 1)
            ends(n_t + 1, 1, n_t // 2, 0)


def build(nc, t, stages=None):
    modulation(nc, t)
    for lay in range(DEPTH):
        with nc.sbuf_tensor(f"h_hi{lay}", [P, KT, TOK], F32R) as h_hi, nc.sbuf_tensor(f"h_lo{lay}", [P, KT, TOK], F32R) as h_lo:
            normalise(nc, t, lay, h_hi, h_lo, t["x_in"] if lay == 0 else t["x_mid"])
            with Mem(nc, f"w{lay}") as m:
                w = Weights(m)
                for project in (project_a, project_qkv, project_c):
                    project(nc, t, lay, (h_hi, h_lo), w)
        if stages == 1:
            return
        gates_and_rotary(nc, t, lay)
        deltanet(nc, t, lay)
        if lay < DEPTH - 1:
            attention(nc, t, lay, True)
        with nc.sbuf_tensor(f"w_hi{lay}", [P, KT, D], F32R) as w_hi, nc.sbuf_tensor(f"w_lo{lay}", [P, KT, D], F32R) as w_lo:
            attention(nc, t, lay, False, w_hi, w_lo)
            finish(nc, t, lay, w_hi, w_lo)
        if stages == 2:
            return


def tiled(w):
    *lead, k, n = w.shape
    w = w.reshape(*lead, k // P, P, n // P, P)
    ax = list(range(len(lead)))
    q = len(lead)
    return np.ascontiguousarray(w.transpose(*ax, q + 2, q + 1, q, q + 3))


def lay_out(a):
    f = {k: np.asarray(v) for k, v in a.items()}
    out = {}
    out["x_in"] = np.concatenate([f["ctx"][0], f["x"][0]], axis=0)
    cond = np.stack([f["c"][0], f["c_ctx"]], axis=-1)
    out["cond"] = np.ascontiguousarray(cond.reshape(KT, P, 2).transpose(1, 0, 2))
    aw = f["ada_w"].reshape(DEPTH, KT, P, 6, 512)
    out["ada_w"] = np.ascontiguousarray(aw.transpose(0, 3, 2, 1, 4).reshape(DEPTH * 6, P, KT, 512))
    out["ada_b"] = np.ascontiguousarray(np.broadcast_to(f["ada_b"][None], (2, DEPTH, 3 * D)))
    out["norm_w"] = np.ascontiguousarray(f["norm_w"].reshape(DEPTH, KT, P).transpose(0, 2, 1))
    q_pairs = [np.r_[j * HD:(j + 1) * HD, (j + 3) * HD:(j + 4) * HD] for j in range(3)]
    z = [512 + np.arange(P), 640 + np.arange(P)] + [1920 + P * i + np.arange(P) for i in range(3)] + [2968 + q for q in q_pairs]
    cols = []
    for c in range(2):
        cols += [P * c + np.arange(P), 256 + P * c + np.arange(P)] + z[4 * c:4 * c + 4]
    for i in range(3):
        cols += [768 + P * i + np.arange(P), 1152 + P * i + np.arange(P), 1536 + P * i + np.arange(P)]
    cols += [2328 + q for q in q_pairs] + [2712 + np.arange(P), 2840 + np.arange(P), 2304 + np.arange(24)]
    w = f["w_in"][:, :, np.concatenate(cols)]
    w = np.concatenate([w, np.zeros((DEPTH, D, NS * P - w.shape[2]), np.float32)], axis=2)
    out["w_in"] = tiled(w)
    ca = np.concatenate([f["conv_a_w"], f["conv_a_b"][:, None]], axis=1)
    out["conv_a"] = np.ascontiguousarray(ca.reshape(DEPTH, CW_A + 1, 2, P).transpose(0, 3, 2, 1))
    cb = f["qkv_conv_w"].reshape(DEPTH, CW_B, 3, 3, P)
    out["conv_b"] = np.ascontiguousarray(cb.transpose(0, 4, 3, 2, 1).reshape(DEPTH, P, 9, CW_B))
    every = lambda x: np.ascontiguousarray(np.broadcast_to(x[:, None], (x.shape[0], P, *x.shape[1:])))
    out["dt_bias"], out["a_log"], out["sink"] = every(f["dt_bias"]), every(f["a_log"]), every(f["sink"])
    out["fnw"] = np.ascontiguousarray(np.broadcast_to(f["final_norm_w"], (P, D)))
    out["ln_w"], out["ln_b"] = (np.ascontiguousarray(f[n].reshape(DEPTH, 2, P).transpose(0, 2, 1)) for n in ("ln_a_w", "ln_a_b"))
    out["dn_w"] = np.ascontiguousarray(np.tile(f["dn_norm_w"], (1, 2))[:, :, None])
    order = np.r_[0:640, np.concatenate([640 + q for q in q_pairs])]
    out["w_out"] = np.ascontiguousarray(f["w_out"][:, order].reshape(DEPTH, KT, P, D).transpose(0, 2, 1, 3))
    out.update(constants())
    return out


def constants():
    c = {}
    c["ident"] = np.eye(P, dtype=np.float32)
    c["blockdiag"] = np.kron(np.eye(2, dtype=np.float32), np.ones((HD, HD), np.float32))
    c["ones"] = np.ones((P, HD), np.float32)
    c["mean_w"] = np.full((P, P), 1.0 / (2 * P), np.float32)
    f = np.arange(P) % HD
    freq = (10000.0 ** (-np.arange(16, dtype=np.float32) / 16)).astype(np.float32)[f % 16]
    pos = np.arange(SEQ)
    where = np.where((f // 32 == 0)[:, None], pos // 64, pos % 64).astype(np.float32)
    ang = where * freq[:, None]
    c["cos"] = np.cos(ang).astype(np.float32)
    c["sin"] = (np.sin(ang) * np.where(f % 32 < 16, -1, 1)[:, None]).astype(np.float32)
    c["swap"] = np.eye(P, dtype=np.float32)[np.arange(P) ^ 16]
    qi, ki = np.arange(P)[:, None], np.arange(P)[None]
    left, right = np.where(ki >= qi, 0, NEG), np.where(ki <= qi, 0, NEG)
    mask = np.stack([np.concatenate([left, right], 1)] * (SEQ // P)).astype(np.float32)
    mask[0, :, :P] = NEG
    mask[-1, :, P:] = NEG
    c["mask"] = mask
    a, b = np.arange(CH)[:, None], np.arange(CH)[None]
    both = lambda fwd: np.concatenate([fwd(a, b), fwd(-a, -b)]).astype(np.float32)
    c["tri_c"] = both(lambda i, j: i <= j)
    c["tri"] = (np.concatenate([c["tri_c"]] * 2, axis=1) * c["blockdiag"]).astype(np.float32)
    c["negmask"] = np.where(c["tri_c"] > 0, 0, NEG).astype(np.float32)
    c["dirmask"] = np.kron(np.eye(2, dtype=np.float32), np.ones((CH, 1), np.float32))
    below = lambda s: np.concatenate([(a // s % 2 == 1) & (b // s == a // s - 1),
                                      (b // s % 2 == 1) & (a // s == b // s - 1)]).astype(np.float32)
    side_by_side = lambda x: np.concatenate([x, x], axis=1) * c["blockdiag"]
    c["lmask"] = np.ascontiguousarray(np.stack([side_by_side(below(s)) + c["ident"] for s in (1, 2, 4, 8, 16, 32)], axis=1))
    c["umask1"] = np.ascontiguousarray(c["lmask"][:, 0].T)
    c["minus_strict"] = -both(lambda i, j: i < j)
    return c


SCRATCH = {
    "gates": (TOK, 4 * NH),
    "qk": (4, P, TOK + KPAD),
    "vt": (NT + 1, P, P),
    "yc": (3, P, TOK),
    "scan": (2, TOK, NH * HD),
    "mod": (DEPTH * 6, 2, 512),
    "rows": (NS, P, RL),
    "x_mid": (TOK, D),
}


def program(nc, shapes, debug=(), stages=None):
    t = {n: nc.dram_tensor(f"in_{n}", shape, F32, kind="ExternalInput").ap() for n, shape in shapes.items()}
    for n, shape in SCRATCH.items():
        t[n] = nc.dram_tensor(n, shape, F32, kind="ExternalOutput" if n in debug else "Internal").ap()
    t["out"] = nc.dram_tensor("out_0", (SEQ, D), F32, kind="ExternalOutput").ap()
    build(nc, t, stages)


def kernel(**inputs):
    import concourse.bacc as _bacc
    from concourse.bass_utils import run_bass_kernel_spmd as _run

    arrays = lay_out(inputs)
    nc = _bacc.Bacc("TRN2", target_bir_lowering=False, num_devices=1)
    program(nc, {n: a.shape for n, a in arrays.items()})
    r = _run(nc, [{f"in_{n}": a for n, a in arrays.items()}], core_ids=[0])
    return r.results[0]["out_0"].reshape(1, SEQ, D)
```
